# Optimizing a Trainium2 kernel written in Bass

```python
import jax, jax.numpy as jnp
from jax import lax
import numpy as np

D_MODEL = 1024
BATCH = 1
SEQ = 1024
DEPTH = 2
DEC_BATCH = 8
DEC_SEQ = 8
PAST_LEN = 256
PAGE_SIZE = 128

N_HEADS_A = 8
HEAD_DIM = 64
WIDTH_A = N_HEADS_A * HEAD_DIM
N_GROUPS_B = 8
GROUP_DIM = 64
WIDTH_B = N_GROUPS_B * GROUP_DIM
CHUNK = 128
Q_BLOCK = 128
EPS = 1e-6
IN_COLS = 4 * WIDTH_A + N_HEADS_A + 3 * WIDTH_B + 2 * D_MODEL

kernel_name = "fox_gmlp_gated_hybrid_step"

def rms_norm(x, g):
    xf = x.astype(jnp.float32)
    r = lax.rsqrt(jnp.mean(xf * xf, axis=-1, keepdims=True) + EPS)
    return (xf * r).astype(x.dtype) * g

def in_proj(h, w_in, b_forget, q_norm_g, k_norm_g, v_norm_g):
    z = h @ w_in
    sizes = (WIDTH_A,) * 4 + (N_HEADS_A,) + (WIDTH_B,) * 3 + (D_MODEL,) * 2
    idx = [int(i) for i in np.cumsum(sizes)[:-1]]
    q, k, v, gate_a, f_logit, u, vb, gate_b, g_a, g_b = jnp.split(z, idx, axis=-1)
    hs = h.shape[:-1] + (N_HEADS_A, HEAD_DIM)
    q = rms_norm(q.reshape(hs), q_norm_g)
    k = rms_norm(k.reshape(hs), k_norm_g)
    v = v.reshape(hs)
    logf = jax.nn.log_sigmoid((f_logit + b_forget).astype(jnp.float32))
    u = jax.nn.gelu(u)
    vb = rms_norm(jax.nn.gelu(vb), v_norm_g)
    return q, k, v, gate_a, logf, u, vb, gate_b, g_a, g_b

def fox_prompt(q, k, v, logf):
    B, S = q.shape[0], q.shape[1]
    c = jnp.cumsum(logf, axis=1).transpose(0, 2, 1)
    scale = HEAD_DIM ** -0.5
    kpos = jnp.arange(S)

    def block(i):
        start = i * Q_BLOCK
        qb = lax.dynamic_slice_in_dim(q, start, Q_BLOCK, axis=1)
        cb = lax.dynamic_slice_in_dim(c, start, Q_BLOCK, axis=2)
        s = jnp.einsum('bqhd,bkhd->bhqk', qb, k).astype(jnp.float32) * scale
        s = s + (cb[..., :, None] - c[..., None, :])
        qpos = start + jnp.arange(Q_BLOCK)
        s = jnp.where(qpos[:, None] >= kpos[None, :], s, -jnp.inf)
        p = jax.nn.softmax(s, axis=-1).astype(v.dtype)
        return jnp.einsum('bhqk,bkhd->bqhd', p, v)

    out = lax.map(block, jnp.arange(S // Q_BLOCK))
    return out.transpose(1, 0, 2, 3, 4).reshape(B, S, N_HEADS_A, HEAD_DIM)

def fox_sample(q, k, v, logf, ck, cv, cl, page_table):
    DB, T = q.shape[0], q.shape[1]
    kp = ck[page_table].reshape(DB, -1, N_HEADS_A, HEAD_DIM)
    vp = cv[page_table].reshape(DB, -1, N_HEADS_A, HEAD_DIM)
    lp = cl[page_table].reshape(DB, -1, N_HEADS_A).astype(jnp.float32)
    P = kp.shape[1]
    c_past = jnp.cumsum(lp, axis=1)
    c_new = c_past[:, -1:, :] + jnp.cumsum(logf, axis=1)
    c_past = c_past.transpose(0, 2, 1)
    c_new = c_new.transpose(0, 2, 1)
    scale = HEAD_DIM ** -0.5
    s_past = jnp.einsum('bqhd,bkhd->bhqk', q, kp).astype(jnp.float32) * scale
    s_past = s_past + (c_new[..., :, None] - c_past[..., None, :])
    s_new = jnp.einsum('bqhd,bkhd->bhqk', q, k).astype(jnp.float32) * scale
    s_new = s_new + (c_new[..., :, None] - c_new[..., None, :])
    tpos = jnp.arange(T)
    s_new = jnp.where(tpos[:, None] >= tpos[None, :], s_new, -jnp.inf)
    p = jax.nn.softmax(jnp.concatenate([s_past, s_new], axis=-1), axis=-1).astype(v.dtype)
    return (jnp.einsum('bhqk,bkhd->bqhd', p[..., :P], vp)
            + jnp.einsum('bhqk,bkhd->bqhd', p[..., P:], v))

def sgu_prompt(vb, w_s, b_s):
    B, S = vb.shape[0], vb.shape[1]
    vc = vb.reshape(B, S // CHUNK, CHUNK, N_GROUPS_B, GROUP_DIM)
    w = w_s * jnp.tril(jnp.ones((CHUNK, CHUNK), w_s.dtype))
    s = jnp.einsum('gts,bnsgd->bntgd', w, vc) + b_s.T[None, None, :, :, None]
    return s.reshape(B, S, WIDTH_B)

def sgu_sample(vb, w_s, b_s):
    DB, T = vb.shape[0], vb.shape[1]
    vc = vb.reshape(DB, T, N_GROUPS_B, GROUP_DIM)
    w = w_s[:, :T, :T] * jnp.tril(jnp.ones((T, T), w_s.dtype))
    s = jnp.einsum('gts,bsgd->btgd', w, vc) + b_s[:, :T].T[None, :, :, None]
    return s.reshape(DB, T, WIDTH_B)

def merge_out(attn, s_sgu, u, gate_a, gate_b, g_a, g_b, w_pa, w_pb, w_o):
    a = attn.reshape(attn.shape[:-2] + (WIDTH_A,)) * jax.nn.silu(gate_a)
    b = u * s_sgu * jax.nn.silu(gate_b)
    m = jax.nn.sigmoid(g_a) * (a @ w_pa) + jax.nn.sigmoid(g_b) * (b @ w_pb)
    return m @ w_o

def setup_inputs(seed: int = 0) -> dict:
    key = jax.random.key(seed)
    ks = jax.random.split(key, 20)
    n_pages = PAST_LEN // PAGE_SIZE
    n_used = DEC_BATCH * n_pages
    n_pool = n_used + n_used // 4
    f32 = jnp.float32
    nrm = lambda k, shape, s: jax.random.normal(k, shape, f32) * s
    page_table = jax.random.permutation(ks[0], n_pool)[:n_used].reshape(DEC_BATCH, n_pages).astype(jnp.int32)
    return {
        "x_prompt": nrm(ks[1], (BATCH, SEQ, D_MODEL), 1.0),
        "x_sample": nrm(ks[2], (DEC_BATCH, DEC_SEQ, D_MODEL), 1.0),
        "cache_k": nrm(ks[3], (DEPTH, n_pool, PAGE_SIZE, N_HEADS_A, HEAD_DIM), 1.0),
        "cache_v": nrm(ks[4], (DEPTH, n_pool, PAGE_SIZE, N_HEADS_A, HEAD_DIM), 1.0),
        "cache_logf": jax.nn.log_sigmoid(3.0 + nrm(ks[5], (DEPTH, n_pool, PAGE_SIZE, N_HEADS_A), 1.0)),
        "page_table": page_table,
        "norm_g": 1.0 + nrm(ks[6], (DEPTH, D_MODEL), 0.05),
        "w_in": nrm(ks[7], (DEPTH, D_MODEL, IN_COLS), D_MODEL ** -0.5),
        "b_forget": 3.0 + nrm(ks[8], (DEPTH, N_HEADS_A), 0.5),
        "q_norm_g": 1.0 + nrm(ks[9], (DEPTH, HEAD_DIM), 0.05),
        "k_norm_g": 1.0 + nrm(ks[10], (DEPTH, HEAD_DIM), 0.05),
        "v_norm_g": 1.0 + nrm(ks[11], (DEPTH, WIDTH_B), 0.05),
        "w_s": nrm(ks[12], (DEPTH, N_GROUPS_B, CHUNK, CHUNK), CHUNK ** -0.5),
        "b_s": 1.0 + nrm(ks[13], (DEPTH, N_GROUPS_B, CHUNK), 0.1),
        "w_proj_a": nrm(ks[14], (DEPTH, WIDTH_A, D_MODEL), WIDTH_A ** -0.5),
        "w_proj_b": nrm(ks[15], (DEPTH, WIDTH_B, D_MODEL), WIDTH_B ** -0.5),
        "w_out": nrm(ks[16], (DEPTH, D_MODEL, D_MODEL), D_MODEL ** -0.5),
    }

def reference(x_prompt, x_sample, cache_k, cache_v, cache_logf, page_table, norm_g, w_in, b_forget,
              q_norm_g, k_norm_g, v_norm_g, w_s, b_s, w_proj_a, w_proj_b, w_out):
    xp, xs = x_prompt, x_sample
    kp_l, vp_l, lp_l, ks_l, vs_l, ls_l, sv_l = [], [], [], [], [], [], []
    for l in range(DEPTH):
        hp = rms_norm(xp, norm_g[l])
        q, k, v, ga, logf, u, vb, gb, g_a, g_b = in_proj(hp, w_in[l], b_forget[l], q_norm_g[l], k_norm_g[l], v_norm_g[l])
        attn = fox_prompt(q, k, v, logf)
        s_sgu = sgu_prompt(vb, w_s[l], b_s[l])
        xp = xp + merge_out(attn, s_sgu, u, ga, gb, g_a, g_b, w_proj_a[l], w_proj_b[l], w_out[l])
        kp_l.append(k)
        vp_l.append(v)
        lp_l.append(logf.astype(cache_logf.dtype))
        hs = rms_norm(xs, norm_g[l])
        q, k, v, ga, logf, u, vb, gb, g_a, g_b = in_proj(hs, w_in[l], b_forget[l], q_norm_g[l], k_norm_g[l], v_norm_g[l])
        attn = fox_sample(q, k, v, logf, cache_k[l], cache_v[l], cache_logf[l], page_table)
        s_sgu = sgu_sample(vb, w_s[l], b_s[l])
        xs = xs + merge_out(attn, s_sgu, u, ga, gb, g_a, g_b, w_proj_a[l], w_proj_b[l], w_out[l])
        ks_l.append(k)
        vs_l.append(v)
        ls_l.append(logf.astype(cache_logf.dtype))
        sv_l.append(vb)
    return (xp, xs, jnp.stack(kp_l), jnp.stack(vp_l), jnp.stack(lp_l),
            jnp.stack(ks_l), jnp.stack(vs_l), jnp.stack(ls_l), jnp.stack(sv_l))


_drawn_inputs = setup_inputs


def setup_inputs(seed=0):
    import zlib

    import numpy as np

    out = dict(_drawn_inputs(seed))
    spreads = {}
    factors = {'cache_logf': 3.064, 'q_norm_g': 8.0}
    for name, (base, spread) in spreads.items():
        noise = np.random.default_rng([zlib.crc32(name.encode()), seed]).standard_normal(out[name].shape)
        drawn = base * np.exp(spread * noise) if base else spread * noise
        out[name] = __import__('jax').numpy.asarray(drawn.astype(out[name].dtype))
    for name, factor in factors.items():
        out[name] = (out[name] * factor).astype(out[name].dtype)
    return out
```

```python
import concourse.bass as bass
from concourse import mybir
from contextlib import ExitStack

F32 = mybir.dt.float32
F32R = mybir.dt.float32r
I32 = mybir.dt.int32
ALU = mybir.AluOpType
ACT = mybir.ActivationFunctionType
AX = mybir.AxisListType

P = 128
D = 1024
KT = D // P
SEQ, DEPTH, DB, DT, PAST = 1024, 2, 8, 8, 256
NS_TOK = DB * DT
NTOK = SEQ + NS_TOK
H, HD = 8, 64
WA = H * HD
PAIRS = H // 2
NT = SEQ // P + 1
PT_ = SEQ // P
ROWS = [P] * PT_ + [NS_TOK]
CHUNKS = [(0, 384), (384, 384), (768, NTOK - 768)]
N_POOL, NPG = 20, PAST // P
EPS = 1e-6
C_Q, C_K, C_V, C_GA = 0, WA, 2 * WA, 3 * WA
C_F = 4 * WA
C_U = C_F + H
C_VB, C_GB = C_U + WA, C_U + 2 * WA
C_MA = C_U + 3 * WA
C_MB = C_MA + D
IN_COLS = C_MB + D
NEG = -float(2.0 ** 100)
GC = 0.044715
GS = 0.7978845608028654


class Region:

    def __init__(self, nc, tag, start):
        self.nc, self.tag, self.at = nc, tag, start

    def __call__(self, name, shape, dt=F32):
        n = 4
        for s in shape[1:]:
            n *= s
        t = self.nc.alloc_sbuf_tensor_at(f"{self.tag}_{name}", shape, dt, offset=self.at)
        self.at += (n + 31) // 32 * 32
        return t


def three(nc, out, pairs, start, stop):
    n = len(pairs)
    for i, (sh, sl, mh, ml) in enumerate(pairs):
        nc.tensor.matmul(out, sh, mh, start=start and i == 0, stop=False)
        nc.tensor.matmul(out, sh, ml, start=False, stop=False)
        last = nc.tensor.matmul(out, sl, mh, start=False, stop=stop and i == n - 1)
    return last


def row(dram2d, t):
    return dram2d[t * P:t * P + ROWS[t], :]


def rows_phase(nc, l, g, project, sem):
    R = Region(nc, "wo" if project else "in", g.free_rows if project else g.free)
    tag = "w" if project else "i"
    S = lambda n: sem(f"{tag}_{n}")
    xt = R("x", [P, 2, D])
    hn = R("hn", [P, 2, D])
    gain = R("gain", [P, D])
    sqj = R("sqj", [P, D])
    ss, ms, rs, ex = R("ss", [P, 2]), R("ms", [P, 2]), R("rs", [P, 2]), R("ex", [P, 1])
    if project:
        NW, NST = 16, 4
        stage, whi, wlo = R("stage", [P, NST, 512]), R("whi", [P, NW, 512], F32R), R("wlo", [P, NW, 512], F32R)
    assert R.at <= g.end, (R.tag, R.at, g.end)
    yps = [[g.bank[0], g.bank[1]], [g.bank[2], g.bank[3]]]
    hps = [[g.bank[4], g.bank[5]], [g.bank[6], g.bank[7]]]
    x_in = [S("x0"), S("x1")]
    y_out = [S("y0"), S("y1")]
    consts = S("consts")
    w_in = [S(f"w{i}") for i in range(4)]
    w_hi, w_lo_p, w_lo_v = S("whi"), S("wlop"), S("wlov")
    m_hi, m_lo, y_ps, y_ready = S("mhi"), S("mlo"), S("yps"), S("yready")
    ss_r, ms_r, rs_r, hn_r, tr_r, h_hi, h_lo, own = (S("ss"), S("ms"), S("rs"), S("hn"), S("tr"), S("hhi"),
                                                    S("hlo"), S("own"))

    def y_rows(t):
        return row(g.yp2, t) if t < PT_ else g.ys2[:, :]

    with nc.Block() as block:
        @block.sync
        def _(sp):
            src = g.gains[0:1, :] if not project else g.gains[bass.ds(l + 1, 1), :]
            sp.dma_start(gain[:, :], src.to_broadcast([P, D])).then_inc(consts, 16)

            def load(t):
                if t >= 2:
                    sp.wait_ge(y_out[t % 2], 16 * (t // 2))
                    sp.wait_ge(hn_r, t - 1)
                    sp.wait_ge(ss_r, t - 1)
                src = y_rows(t) if project else (row(g.xp2, t) if t < PT_ else g.xs2[:, :])
                sp.dma_start(xt[0:ROWS[t], t % 2, :], src).then_inc(x_in[t % 2], 16)

            if project:
                for u in range(NW):
                    half, k = divmod(u, KT)
                    if u >= NST:
                        sp.wait_ge(w_hi, u - NST + 1)
                        sp.wait_ge(w_lo_p, (u - NST) // 2 + 1)
                        sp.wait_ge(w_lo_v, (u - NST + 1) // 2)
                    sp.dma_start(stage[:, u % NST, :],
                                 g.w_out[bass.ds(l, 1), k * P:(k + 1) * P, half * 512:half * 512 + 512]
                                 .rearrange("a p n -> (a p) n")).then_inc(w_in[u % NST], 16)
                    if u in (4, 6):
                        load((u - 4) // 2)
            else:
                load(0)
                load(1)
            for t in range(NT):
                if project:
                    sp.wait_ge(y_ready, t + 1)
                else:
                    sp.wait_ge(x_in[t % 2], 16 * (t // 2 + 1))
                sp.dma_start(y_rows(t), xt[0:ROWS[t], t % 2, :]).then_inc(y_out[t % 2], 16)
                if t + 2 < NT:
                    load(t + 2)
            sp.wait_ge(y_out[0], 16 * ((NT + 1) // 2))
            sp.wait_ge(y_out[1], 16 * (NT // 2))

        @block.scalar
        def _(act):
            def split_m(t):
                r = slice(t * P, t * P + ROWS[t])
                nc.scalar.activation(g.h_hi[:, :, r], g.m[:, :, r], ACT.Copy, scale=0.5).then_inc(m_hi, 1)

            def split_w(u):
                act.wait_ge(w_in[u % 4], 16 * (u // 4 + 1))
                nc.scalar.activation(whi[:, u, :], stage[:, u % 4, :], ACT.Copy).then_inc(w_hi, 1)

            def evac(t):
                for b in range(2):
                    act.wait_ge(tr_r, t + 1)
                    nc.scalar.activation(g.h_hi[:, 4 * b:4 * b + 4, t * P:t * P + ROWS[t]],
                                         hps[t % 2][b][:, :].rearrange("p (k r) -> p k r", k=4)[:, :, 0:ROWS[t]],
                                         ACT.Copy).then_inc(h_hi, 1)

            if project:
                split_m(0)
                for u in range(8):
                    split_w(u)
                split_m(1)
                for u in range(8, 16):
                    split_w(u)
            for t in range(NT):
                if project and t + 2 < NT:
                    split_m(t + 2)
                if project:
                    act.wait_ge(y_ready, t + 1)
                else:
                    act.wait_ge(x_in[t % 2], 16 * (t // 2 + 1))
                if t:
                    act.wait_ge(ss_r, t)
                    if t >= 2:
                        act.wait_ge(ms_r, t - 1)
                nc.scalar.activation(sqj[0:ROWS[t], :], xt[0:ROWS[t], t % 2, :], ACT.Square,
                                     accum_out=ss[0:ROWS[t], t % 2:t % 2 + 1]).then_inc(ss_r, 1)
                if t:
                    evac(t - 1)
            evac(NT - 1)

        @block.gpsimd
        def _(pool):
            nc.gpsimd.memset(ex[:, :], -0.5).then_inc(own, 1)
            pool.wait_ge(own, 1)
            if project:
                for u in range(0, NW, 2):
                    pool.wait_ge(w_hi, u + 1)
                    nc.gpsimd.tensor_tensor(wlo[:, u, :], stage[:, u % NST, :], whi[:, u, :].bitcast(F32),
                                            ALU.subtract).then_inc(w_lo_p, 1)
            for t in range(NT):
                pool.wait_ge(ms_r, t + 1)
                if t >= 2:
                    pool.wait_ge(hn_r, t - 1)
                nc.gpsimd.tensor_tensor(rs[0:ROWS[t], t % 2:t % 2 + 1], ms[0:ROWS[t], t % 2:t % 2 + 1],
                                        ex[0:ROWS[t], :], ALU.pow).then_inc(rs_r, 1)

        @block.vector
        def _(dve):
            def split_m(t):
                r = slice(t * P, t * P + ROWS[t])
                dve.wait_ge(m_hi, t + 1)
                nc.vector.scalar_tensor_tensor(g.h_lo[:, :, r], g.m[:, :, r], 0.5, g.h_hi[:, :, r].bitcast(F32),
                                               ALU.mult, ALU.subtract).then_inc(m_lo, 1)

            def evac(t):
                for b in range(2):
                    r = slice(t * P, t * P + ROWS[t])
                    dve.wait_ge(h_hi, 2 * t + b + 1)
                    nc.vector.tensor_tensor(g.h_lo[:, 4 * b:4 * b + 4, r],
                                            hps[t % 2][b][:, :].rearrange("p (k r) -> p k r", k=4)[:, :, 0:ROWS[t]],
                                            g.h_hi[:, 4 * b:4 * b + 4, r].bitcast(F32),
                                            ALU.subtract).then_inc(h_lo, 1)

            if project:
                split_m(0)
                for u in range(1, NW, 2):
                    dve.wait_ge(w_hi, u + 1)
                    nc.vector.tensor_tensor(wlo[:, u, :], stage[:, u % NST, :], whi[:, u, :].bitcast(F32),
                                            ALU.subtract).then_inc(w_lo_v, 1)
                    if u == 7:
                        split_m(1)
            dve.wait_ge(consts, 16)
            for t in range(NT):
                n = ROWS[t]
                if project:
                    dve.wait_ge(x_in[t % 2], 16 * (t // 2 + 1))
                    dve.wait_ge(y_ps, t + 1)
                    for b in range(2):
                        cols = slice(512 * b, 512 * b + 512)
                        last = nc.vector.tensor_tensor(xt[0:n, t % 2, cols], yps[t % 2][b][0:n, :],
                                                       xt[0:n, t % 2, cols], ALU.add)
                    last.then_inc(y_ready, 1)
                    if t + 2 < NT:
                        split_m(t + 2)
                if t:
                    evac(t - 1)
                dve.wait_ge(ss_r, t + 1)
                if t >= 2:
                    dve.wait_ge(rs_r, t - 1)
                nc.vector.tensor_scalar(ms[0:n, t % 2:t % 2 + 1], ss[0:n, t % 2:t % 2 + 1], 1.0 / D, EPS,
                                        ALU.mult, ALU.add).then_inc(ms_r, 1)
                dve.wait_ge(rs_r, t + 1)
                if t >= 2:
                    dve.wait_ge(tr_r, t - 1)
                nc.vector.scalar_tensor_tensor(hn[0:n, t % 2, :], xt[0:n, t % 2, :], rs[0:n, t % 2:t % 2 + 1],
                                               gain[0:n, :], ALU.mult, ALU.mult).then_inc(hn_r, 1)
            evac(NT - 1)

        @block.tensor
        def _(pe):
            def transposes(t):
                pe.wait_ge(hn_r, t + 1)
                if t >= 2:
                    pe.wait_ge(h_lo, 2 * (t - 1))
                for k in range(KT):
                    last = nc.tensor.transpose(hps[t % 2][k // 4][:, (k % 4) * P:(k % 4) * P + ROWS[t]],
                                               hn[0:ROWS[t], t % 2, k * P:(k + 1) * P],
                                               g.ident[0:ROWS[t], 0:ROWS[t]])
                last.then_inc(tr_r, 1)

            for t in range(NT):
                if project:
                    r = slice(t * P, t * P + ROWS[t])
                    pe.wait_ge(m_lo, t + 1)
                    if t >= 2:
                        pe.wait_ge(y_ready, t - 1)
                    for half in range(2):
                        for k in range(KT):
                            u = half * KT + k
                            if t == 0:
                                if u % 2:
                                    pe.wait_ge(w_lo_v, u // 2 + 1)
                                else:
                                    pe.wait_ge(w_lo_p, u // 2 + 1)
                            last = three(nc, yps[t % 2][half][0:ROWS[t], :],
                                         [(g.h_hi[:, k, r], g.h_lo[:, k, r], whi[:, u, :], wlo[:, u, :])],
                                         k == 0, k == KT - 1)
                    last.then_inc(y_ps, 1)
                    if t:
                        transposes(t - 1)
                else:
                    transposes(t)
            if project:
                transposes(NT - 1)


LAG = 2


def attention_plan():
    plan = [("L", 0)] + [("W", 0, k) for k in range(KT)]
    for t in range(NT):
        if t == NT - 1:
            plan.append(("L", 1))
        plan.append(("Z", 0, t))
        if t:
            plan.append(("X", 0, t - 1))
    plan += [("W", 1, k) for k in range(KT)]
    plan += [("X", 0, NT - 1), ("F",), ("Z", 1, 0), ("Z", 1, 1), ("X", 1, 0), ("C",), ("N", 0),
             ("Z", 1, 2), ("X", 1, 1), ("Z", 1, 3), ("X", 1, 2)]
    plan += [("S", 0, i) for i in range(4)] + [("X", 1, 3)]
    after = {}
    PER = 12

    def put(n, *steps):
        after.setdefault(n, []).extend(steps)

    for h in range(H):
        if h:
            put(PER * (h - 1), ("N", h))
        for i, off in enumerate((-10, -9, -8, -6, -4, -3, -2, 0)):
            if h or i >= 4:
                put(max(0, PER * h + off), ("S", h, i))
    for p in range(1, PAIRS):
        at = [2, 6, 10, 14, 18] if p == 1 else [3, 5, 7, 9, 11, 13, 15, 17, 19]
        for t, n in zip(range(NT - len(at), NT), at):
            n += 2 * PER * (p - 1)
            if t == NT - 1 and p + 1 < PAIRS:
                put(n - 1, ("L", p + 1))
            put(n, ("Z", p, t))
            if t and ("X", p, t - 1) not in plan:
                put(n, ("X", p, t - 1))
        put(n + 1, ("X", p, NT - 1))
        if p + 1 < PAIRS:
            for k in range(KT):
                put(n + 1 + k // 2, ("W", p + 1, k))
    steps = [(h, G, j) for h in range(H) for G in range(2) for j in range(4 * G + 4)]
    for n in range(len(steps) + LAG):
        if n < len(steps):
            plan.append(("T",) + steps[n])
        if n >= LAG:
            plan.append(("V",) + steps[n - LAG])
            h, G, j = steps[n - LAG]
            if j == 4 * G + 3:
                plan.append(("O", h, G))
        plan += after.pop(n, [])
    assert not after
    return plan


def attention_phase(nc, l, g, sem):
    plan = attention_plan()
    R = Region(nc, "at", g.free_attention)
    S = lambda n: sem(f"a_{n}")
    WID = 3 * P + H
    NW, NST = KT, 4
    stage = R("stage", [P, NST, WID])
    whi, wlo = R("whi", [P, NW, WID], F32R), R("wlo", [P, NW, WID], F32R)
    qk_hi, qk_lo = R("qkhi", [P, 2, 2, SEQ], F32R), R("qklo", [P, 2, 2, SEQ], F32R)
    v_hi, v_lo = R("vhi", [P, 2, PT_, P], F32R), R("vlo", [P, 2, PT_, P], F32R)
    NBLK = PT_ * (PT_ + 1) // 2
    prob = R("prob", [P, NBLK * P])
    pt_hi, pt_lo = R("pthi", [P, LAG + 1, 512], F32R), R("ptlo", [P, LAG + 1, 512], F32R)
    decay = R("decay", [P, SEQ])
    zc, qn = R("zc", [P, 2, 3 * P]), R("qn", [P, 2, 2 * P])
    sq, zg, gqk = R("sq", [P, 2 * P]), R("zg", [P, 2 * P]), R("gqk", [P, 2 * P])
    ssum, ms, rs, ex = R("ssum", [P, 4]), R("ms", [P, 4]), R("rs", [P, 4]), R("ex", [P, 4])
    mx, nmx, sm, rc = R("mx", [P, 4]), R("nmx", [P, 2]), R("sm", [P, 2]), R("rc", [P, 2])
    bf, ff = R("bf", [P, H]), R("ff", [P, NT * H])
    f1, f2, f3, f4 = (R(f"f{i}", [P, NT * H]) for i in range(4))
    assert R.at <= g.end, (R.at, g.end)
    zps, sps, tps, ops, xps = g.bank[0:2], g.bank[2:4], g.bank[4:6], g.bank[6], g.bank[7]
    ncum = prob[0:H, 0:SEQ]
    ones = prob[0:H, SEQ:2 * SEQ]

    order, chunk_at, nchunk = {}, {}, 0
    count = {}
    for s in plan:
        order[s] = count.get(s[0], 0)
        count[s[0]] = order[s] + 1
        if s[0] == "S":
            chunk_at[s] = nchunk
            nchunk += (s[2] + 4) // 4
    xlo_before, vlo_before, n = {}, {}, 0
    for s in plan:
        if s[0] == "X":
            n += s[2] < PT_
            xlo_before[s] = n
    n = 0
    for s in plan:
        if s[0] == "Z":
            n += s[2] < PT_
            vlo_before[s] = n

    consts, gq_r = S("consts"), S("gq")
    w_in = [S(f"w{i}") for i in range(NST)]
    w_hi, w_lo_p, w_lo_v, w_used = S("whi"), S("wlop"), S("wlov"), S("wused")
    z_ready, z_copied, vhi_r, vlo_r, z_free, qn_r = S("z"), S("zc"), S("vhi"), S("vlo"), S("zfree"), S("qn")
    ms_r, kv_out = S("ms"), [S("kv0"), S("kv1")]
    x_ready, x_hi, x_lo = S("x"), S("xhi"), S("xlo")
    f_ready, f_abs, f_exp, f_u, f_ln, f_done, f_out = S("f"), S("fabs"), S("fexp"), S("fu"), S("fln"), S("fd"), S("fo")
    c_ps, c_done, c_out, n_in = S("cps"), S("cd"), S("co"), S("nin")
    s_ready, s_taken, e_bias, e_done, p_ready = S("s"), S("st"), S("eb"), S("ed"), S("p")
    t_ready, t_hi, t_lo, v_done, o_done = S("t"), S("thi"), S("tlo"), S("v"), S("od")
    dve_own, pool_own = S("dve"), S("pool")

    def blk(i):
        return i * (i + 1) // 2 * P

    def before(kind, pair):
        heads = 2 * (pair + 1)
        return {"S": lambda: sum((i + 4) // 4 for i in range(PT_)) * heads,
                "V": lambda: 12 * heads}[kind]()

    def wait_split(eng, u):
        eng.wait_ge(w_lo_v if u % 2 else w_lo_p, u // 2 + 1)

    with nc.Block() as block:
        @block.sync
        def _(sp):
            for i, src in enumerate((g.q_norm_g, g.k_norm_g)):
                for h in range(2):
                    at = i * P + h * HD
                    sp.dma_start(gqk[:, at:at + HD],
                                 src[bass.ds(l, 1), :].to_broadcast([P, HD])).then_inc(consts, 16)
            sp.dma_start(bf[:, :], g.b_forget[bass.ds(l, 1), :].to_broadcast([P, H])).then_inc(consts, 16)

            def load_w(p):
                for k in range(KT):
                    u = p * KT + k
                    if u >= NST:
                        wait_split(sp, u - NST)
                    src = g.w_in[bass.ds(l, 1), k * P:(k + 1) * P, :].rearrange("a p n -> (a p) n")
                    sp.dma_start(stage[:, u % NST, 0:3 * P].rearrange("p (s n) -> p s n", s=3),
                                 src[:, 0:3 * WA].rearrange("p (s n) -> p s n", s=3)[:, :, p * P:(p + 1) * P])\
                      .then_inc(w_in[u % NST], 16)
                    sp.dma_start(stage[:, u % NST, 3 * P:WID], src[:, C_F:C_F + H]).then_inc(w_in[u % NST], 16)

            for s in plan:
                if s[0] == "L":
                    load_w(s[1])
                elif s[0] == "Z":
                    p, t = s[1:]
                    zi, n = order[s], ROWS[t]
                    if t < PT_:
                        k_out = g.nkp[bass.ds(l, 1), t * P:(t + 1) * P, p * P:(p + 1) * P]
                        v_out = g.nvp[bass.ds(l, 1), t * P:(t + 1) * P, p * P:(p + 1) * P]
                    else:
                        k_out = g.nks[bass.ds(l, 1), :, p * P:(p + 1) * P]
                        v_out = g.nvs[bass.ds(l, 1), :, p * P:(p + 1) * P]
                    sp.wait_ge(z_copied, zi + 1)
                    sp.dma_start(v_out.rearrange("a p n -> (a p) n"),
                                 zc[0:n, zi % 2, 2 * P:3 * P]).then_inc(kv_out[zi % 2], 16)
                    sp.wait_ge(qn_r, zi + 1)
                    sp.dma_start(k_out.rearrange("a p n -> (a p) n"),
                                 qn[0:n, zi % 2, P:2 * P]).then_inc(kv_out[zi % 2], 16)
                elif s[0] == "F":
                    sp.wait_ge(f_done, 1)
                    sp.dma_start(g.nlp[bass.ds(l, 1), :, :].rearrange("a (t p) h -> p (a t) h", p=P),
                                 g.logf[:, 0:PT_, :]).then_inc(f_out, 16)
                    sp.dma_start(g.nls[bass.ds(l, 1), :, :].rearrange("a p h -> (a p) h"),
                                 g.logf[0:NS_TOK, PT_, :]).then_inc(f_out, 16)
                elif s[0] == "C":
                    sp.wait_ge(c_done, 2)
                    sp.dma_start(g.ncum_dram[:, :], ncum).then_inc(c_out, 16)
                    sp.wait_ge(c_out, 16)
                elif s[0] == "N":
                    h = s[1]
                    if h:
                        sp.wait_ge(s_taken, before("S", 0) // 2 * h)
                    sp.dma_start(decay[:, :], g.ncum_dram[h:h + 1, :].to_broadcast([P, SEQ])).then_inc(n_in, 16)
            last = count["Z"]
            sp.wait_ge(kv_out[0], 32 * ((last + 1) // 2))
            sp.wait_ge(kv_out[1], 32 * (last // 2))
            sp.wait_ge(f_out, 32)

        @block.scalar
        def _(act):
            for s in plan:
                kind = s[0]
                if s == ("Z", 0, 0):
                    act.wait_ge(consts, 80)
                    nc.scalar.activation(gqk[:, 0:P], gqk[:, 0:P], ACT.Copy, scale=HD ** -0.5).then_inc(gq_r, 1)
                if kind == "W":
                    p, k = s[1:]
                    u = p * KT + k
                    act.wait_ge(w_in[u % NST], 32 * (u // NST + 1))
                    if p and k < KT - 1:
                        act.wait_ge(w_used, (KT - 1) * (p - 1) + k + 1)
                    elif p:
                        act.wait_ge(z_ready, NT * p)
                    nc.scalar.activation(whi[:, k, :], stage[:, u % NST, :], ACT.Copy).then_inc(w_hi, 1)
                elif kind == "Z":
                    p, t = s[1:]
                    zi, n = order[s], ROWS[t]
                    act.wait_ge(z_ready, zi + 1)
                    if zi >= 2:
                        act.wait_ge(kv_out[zi % 2], 32 * (zi // 2))
                        act.wait_ge(z_free, zi - 1)
                    nc.scalar.activation(zc[0:n, zi % 2, :], zps[zi % 2][0:n, 0:3 * P], ACT.Copy).then_inc(z_copied, 1)
                    if t < PT_:
                        if p >= 2:
                            act.wait_ge(v_done, before("V", p - 2))
                        nc.scalar.activation(v_hi[:, p % 2, t, :], zps[zi % 2][:, 2 * P:3 * P], ACT.Copy).then_inc(vhi_r, 1)
                    else:
                        nc.scalar.activation(g.v_s[:, p * P:(p + 1) * P], zps[zi % 2][0:n, 2 * P:3 * P],
                                             ACT.Copy).then_inc(vhi_r, 1)
                elif kind == "X":
                    p, t = s[1:]
                    xi = order[s]
                    act.wait_ge(x_ready, xi + 1)
                    both = xps[:, 0:2 * P].rearrange("p (s r) -> p s r", s=2)
                    if t < PT_:
                        if p >= 2:
                            act.wait_ge(s_ready, before("S", p - 2))
                        nc.scalar.activation(qk_hi[:, p % 2, :, t * P:(t + 1) * P], both, ACT.Copy).then_inc(x_hi, 1)
                    else:
                        nc.scalar.activation(g.qk_s[:, :, p, :], both[:, :, 0:NS_TOK], ACT.Copy).then_inc(x_hi, 1)
                elif kind == "F":
                    act.wait_ge(f_abs, 1)
                    nc.scalar.activation(f2[:, :], f1[:, :], ACT.Exp).then_inc(f_exp, 1)
                    act.wait_ge(f_u, 1)
                    nc.scalar.activation(f4[:, :], f3[:, :], ACT.Ln).then_inc(f_ln, 1)
                elif kind == "S":
                    h, i = s[1:]
                    si = order[s]
                    w = (i + 1) * P
                    act.wait_ge(e_bias, si + 1)
                    if si >= 2:
                        act.wait_ge(p_ready, si - 1)
                    nc.scalar.activation(prob[:, blk(i):blk(i) + w], prob[:, blk(i):blk(i) + w], ACT.Exp,
                                         bias=nmx[:, si % 2:si % 2 + 1],
                                         accum_out=sm[:, si % 2:si % 2 + 1]).then_inc(e_done, 1)
                elif kind == "T":
                    h, G, j = s[1:]
                    ti = order[s]
                    lo = max(0, j - 4 * G) * P
                    act.wait_ge(t_ready, ti + 1)
                    if ti > LAG:
                        act.wait_ge(v_done, ti - LAG)
                    nc.scalar.activation(pt_hi[:, ti % (LAG + 1), lo:512], tps[ti % 2][:, lo:512], ACT.Copy).then_inc(t_hi, 1)
                elif kind == "O":
                    h, G = s[1:]
                    q = slice(HD * (h % 2), HD * (h % 2) + HD)
                    act.wait_ge(v_done, order[("V", h, G, 4 * G + 3)] + 1)
                    nc.scalar.activation(g.a[q, h // 2, 512 * G:512 * G + 512], ops[q, :], ACT.Copy).then_inc(o_done, 1)

        @block.gpsimd
        def _(pool):
            own = [0]

            def link(ins):
                own[0] += 1
                ins.then_inc(pool_own, 1)
                pool.wait_ge(pool_own, own[0])

            link(nc.gpsimd.memset(ex[:, :], -0.5))
            for s in plan:
                if s == ("Z", 0, 0):
                    pool.wait_ge(gq_r, 1)
                if s[0] == "W":
                    p, k = s[1:]
                    if not k % 2:
                        pool.wait_ge(w_hi, p * KT + k + 1)
                        nc.gpsimd.tensor_tensor(wlo[:, k, :], stage[:, k % NST, :], whi[:, k, :].bitcast(F32),
                                                ALU.subtract).then_inc(w_lo_p, 1)
                elif s[0] == "Z":
                    p, t = s[1:]
                    zi, n = order[s], ROWS[t]
                    pool.wait_ge(z_copied, zi + 1)
                    if zi:
                        pool.wait_ge(qn_r, zi)
                    link(nc.gpsimd.tensor_tensor(zg[0:n, :], zc[0:n, zi % 2, 0:2 * P], gqk[0:n, :], ALU.mult))
                    pool.wait_ge(ms_r, zi + 1)
                    link(nc.gpsimd.tensor_tensor(rs[0:n, :], ms[0:n, :], ex[0:n, :], ALU.pow))
                    if zi >= 2:
                        pool.wait_ge(kv_out[zi % 2], 32 * (zi // 2))
                        pool.wait_ge(x_ready, min(zi - 1, count["X"]))
                    nc.gpsimd.tensor_tensor(qn[0:n, zi % 2, :].rearrange("p (s d) -> p s d", d=HD),
                                            zg[0:n, :].rearrange("p (s d) -> p s d", d=HD),
                                            rs[0:n, :].unsqueeze(2).to_broadcast([n, 4, HD]),
                                            ALU.mult).then_inc(qn_r, 1)

        s_steps = [s for s in plan if s[0] == "S"]
        normed = set()

        def norm(dve, link, si):
            if si < 0 or si in normed:
                return
            normed.add(si)
            i = s_steps[si][2]
            w = (i + 1) * P
            dve.wait_ge(e_done, si + 1)
            link(nc.vector.reciprocal(rc[:, si % 2:si % 2 + 1], sm[:, si % 2:si % 2 + 1]))
            nc.vector.tensor_scalar(prob[:, blk(i):blk(i) + w], prob[:, blk(i):blk(i) + w],
                                    rc[:, si % 2:si % 2 + 1], None, ALU.mult).then_inc(p_ready, 1)

        @block.vector
        def _(dve):
            own = [0]

            def link(ins):
                own[0] += 1
                ins.then_inc(dve_own, 1)
                dve.wait_ge(dve_own, own[0])

            link(nc.vector.memset(ff[:, :], 0.0))
            scored = 0
            for n, s in enumerate(plan):
                kind = s[0]
                if n and plan[n - 1][0] != "S":
                    norm(dve, link, scored - 1)
                if kind == "W":
                    p, k = s[1:]
                    if k % 2:
                        dve.wait_ge(w_hi, p * KT + k + 1)
                        nc.vector.tensor_tensor(wlo[:, k, :], stage[:, k % NST, :], whi[:, k, :].bitcast(F32),
                                                ALU.subtract).then_inc(w_lo_v, 1)
                elif kind == "Z":
                    if s == ("Z", 0, 0):
                        dve.wait_ge(consts, 80)
                    p, t = s[1:]
                    zi, n = order[s], ROWS[t]
                    z = zps[zi % 2]
                    dve.wait_ge(z_copied, zi + 1)
                    dve.wait_ge(vhi_r, zi + 1)
                    if p == 0:
                        nc.vector.tensor_tensor(ff[0:n, t * H:(t + 1) * H], z[0:n, 3 * P:WID], bf[0:n, :],
                                                ALU.add).then_inc(f_ready, 1)
                    if t < PT_:
                        nc.vector.tensor_tensor(v_lo[:, p % 2, t, :], z[:, 2 * P:3 * P],
                                                v_hi[:, p % 2, t, :].bitcast(F32), ALU.subtract).then_inc(vlo_r, 1)
                    nc.vector.tensor_tensor(sq[0:n, :], z[0:n, 0:2 * P], zc[0:n, zi % 2, 0:2 * P],
                                            ALU.mult).then_inc(z_free, 1)
                    dve.wait_ge(z_free, zi + 1)
                    link(nc.vector.tensor_reduce(ssum[0:n, :], sq[0:n, :].rearrange("p (s d) -> p s d", d=HD),
                                                 axis=AX.X, op=ALU.add))
                    if zi:
                        dve.wait_ge(qn_r, zi)
                    nc.vector.tensor_scalar(ms[0:n, :], ssum[0:n, :], 1.0 / HD, EPS, ALU.mult, ALU.add).then_inc(ms_r, 1)
                elif kind == "X":
                    p, t = s[1:]
                    if t < PT_:
                        dve.wait_ge(x_hi, order[s] + 1)
                        nc.vector.tensor_tensor(qk_lo[:, p % 2, :, t * P:(t + 1) * P],
                                                xps[:, 0:2 * P].rearrange("p (s r) -> p s r", s=2),
                                                qk_hi[:, p % 2, :, t * P:(t + 1) * P].bitcast(F32),
                                                ALU.subtract).then_inc(x_lo, 1)
                elif kind == "F":
                    dve.wait_ge(f_ready, NT)
                    nc.vector.scalar_tensor_tensor(f1[:, :], ff[:, :], -1.0, ff[:, :], ALU.mult, ALU.min).then_inc(f_abs, 1)
                    dve.wait_ge(f_exp, 1)
                    nc.vector.tensor_scalar(f3[:, :], f2[:, :], 1.0, None, ALU.add).then_inc(f_u, 1)
                    dve.wait_ge(f_u, 1)
                    dve.wait_ge(f_ln, 1)
                    link(nc.vector.tensor_scalar(f1[:, :], f3[:, :], -1.0, 1e-30, ALU.add, ALU.add))
                    link(nc.vector.reciprocal(f3[:, :], f1[:, :]))
                    link(nc.vector.scalar_tensor_tensor(f1[:, :], f4[:, :], 1e-30, f2[:, :], ALU.add, ALU.mult))
                    link(nc.vector.tensor_tensor(f4[:, :], f1[:, :], f3[:, :], ALU.mult))
                    nc.vector.scalar_tensor_tensor(g.logf[:, :, :].rearrange("p t h -> p (t h)"), ff[:, :], 0.0,
                                                   f4[:, :], ALU.min, ALU.subtract).then_inc(f_done, 1)
                    link(nc.vector.memset(ones, 1.0))
                elif kind == "C":
                    dve.wait_ge(c_ps, 1)
                    for c in range(2):
                        nc.vector.tensor_tensor_scan(ncum[:, 512 * c:512 * c + 512], ones[:, 0:512], sps[c][0:H, :],
                                                     0.0 if c == 0 else ncum[:, 511:512],
                                                     ALU.mult, ALU.subtract).then_inc(c_done, 1)
                        dve.wait_ge(c_done, c + 1)
                elif kind == "S":
                    h, i = s[1:]
                    si = order[s]
                    G = i // 4
                    nch = (i + 4) // 4
                    if h:
                        dve.wait_ge(t_ready, order[("T", h - 1, G, i)] + 1)
                    if i == 0:
                        dve.wait_ge(n_in, 16 * (h + 1))
                        if s == ("S", 0, 0):
                            dve.wait_ge(c_out, 16)
                    if si >= 2:
                        dve.wait_ge(e_done, si - 1)
                    for c in range(nch):
                        cc = chunk_at[s] + c
                        w = min(512, (i + 1) * P - 512 * c)
                        m = 2 * (si % 2) + c
                        dve.wait_ge(s_ready, cc + 1)
                        nc.vector.tensor_tensor_reduce(
                            out=prob[:, blk(i) + 512 * c:blk(i) + 512 * c + w], in0=sps[cc % 2][:, 0:w],
                            in1=decay[:, 512 * c:512 * c + w], scale=1.0,
                            scalar=-3.0e38 if c == 0 else mx[:, m - 1:m], op0=ALU.add, op1=ALU.max,
                            accum_out=mx[:, m:m + 1]).then_inc(s_taken, 1)
                        dve.wait_ge(s_taken, cc + 1)
                    m = 2 * (si % 2) + nch - 1
                    nc.vector.tensor_scalar(nmx[:, si % 2:si % 2 + 1], mx[:, m:m + 1], -1.0, None,
                                            ALU.mult).then_inc(e_bias, 1)
                    norm(dve, link, si - 1)
                    scored = si + 1
                elif kind == "T":
                    h, G, j = s[1:]
                    ti = order[s]
                    lo = max(0, j - 4 * G) * P
                    dve.wait_ge(t_hi, ti + 1)
                    nc.vector.tensor_tensor(pt_lo[:, ti % (LAG + 1), lo:512], tps[ti % 2][:, lo:512],
                                            pt_hi[:, ti % (LAG + 1), lo:512].bitcast(F32), ALU.subtract).then_inc(t_lo, 1)

        @block.tensor
        def _(pe):
            for s in plan:
                kind = s[0]
                if kind == "Z":
                    p, t = s[1:]
                    zi, n = order[s], ROWS[t]
                    r = slice(t * P, t * P + n)
                    wide = WID if p == 0 else 3 * P
                    if zi >= 2:
                        pe.wait_ge(z_free, zi - 1)
                    for k in range(KT):
                        if t == 0:
                            wait_split(pe, p * KT + k)
                        last = three(nc, zps[zi % 2][0:n, 0:wide],
                                     [(g.h_hi[:, k, r], g.h_lo[:, k, r], whi[:, k, 0:wide], wlo[:, k, 0:wide])],
                                     k == 0, k == KT - 1)
                        if t == NT - 1 and k < KT - 1:
                            last.then_inc(w_used, 1)
                    last.then_inc(z_ready, 1)
                elif kind == "X":
                    p, t = s[1:]
                    xi, n = order[s], ROWS[t]
                    zi = order[("Z", p, t)]
                    pe.wait_ge(qn_r, zi + 1)
                    if xi:
                        pe.wait_ge(x_hi, xi)
                        pe.wait_ge(x_lo, xlo_before[s] - (t < PT_))
                    for i in range(2):
                        last = nc.tensor.transpose(xps[:, i * P:i * P + n], qn[0:n, zi % 2, i * P:(i + 1) * P],
                                                   g.ident[0:n, 0:n])
                    last.then_inc(x_ready, 1)
                elif kind == "C":
                    pe.wait_ge(f_done, 1)
                    for t in range(PT_):
                        last = nc.tensor.transpose(sps[t // 4][0:H, (t % 4) * P:(t % 4 + 1) * P],
                                                   g.logf[:, t, :], g.ident[:, :])
                    last.then_inc(c_ps, 1)
                elif kind == "S":
                    h, i = s[1:]
                    b = (h // 2) % 2
                    hp = slice(HD * (h % 2), HD * (h % 2) + HD)
                    q = slice(i * P, (i + 1) * P)
                    pe.wait_ge(x_lo, xlo_before[("X", h // 2, i)])
                    if s == ("S", 0, 0):
                        pe.wait_ge(c_done, 2)
                    for c in range((i + 4) // 4):
                        cc = chunk_at[s] + c
                        w = min(512, (i + 1) * P - 512 * c)
                        ks = slice(512 * c, 512 * c + w)
                        if cc >= 2:
                            pe.wait_ge(s_taken, cc - 1)
                        diagonal = 512 * c + w == (i + 1) * P
                        last = three(nc, sps[cc % 2][:, 0:w],
                                     [(qk_hi[hp, b, 0, q], qk_lo[hp, b, 0, q], qk_hi[hp, b, 1, ks], qk_lo[hp, b, 1, ks])],
                                     True, not diagonal)
                        if diagonal:
                            last = nc.tensor.matmul(sps[cc % 2][:, w - P:w], g.ident_r[:, :], g.mask_r[:, :],
                                                    start=False, stop=True)
                        last.then_inc(s_ready, 1)
                elif kind == "T":
                    h, G, j = s[1:]
                    ti = order[s]
                    first = max(0, j - 4 * G)
                    pe.wait_ge(p_ready, order[("S", h, 4 * G + 3)] + 1)
                    if ti >= 2:
                        pe.wait_ge(t_lo, ti - 1)
                    for r in range(first, 4):
                        at = blk(4 * G + r) + j * P
                        last = nc.tensor.transpose(tps[ti % 2][:, r * P:(r + 1) * P], prob[:, at:at + P], g.ident[:, :])
                    last.then_inc(t_ready, 1)
                elif kind == "V":
                    h, G, j = s[1:]
                    ti = order[("T", h, G, j)]
                    b = (h // 2) % 2
                    lo = max(0, j - 4 * G) * P
                    end = 4 * G + 3
                    pe.wait_ge(vlo_r, vlo_before[("Z", h // 2, j)])
                    pe.wait_ge(t_lo, ti + 1)
                    if j == 0 and 2 * h + G:
                        pe.wait_ge(o_done, 2 * h + G)
                    last = three(nc, ops[:, lo:512],
                                 [(v_hi[:, b, j, :], v_lo[:, b, j, :], pt_hi[:, ti % (LAG + 1), lo:512], pt_lo[:, ti % (LAG + 1), lo:512])],
                                 j == 0, j == end)
                    last.then_inc(v_done, 1)


def split_units(nc, eng, u, stage, whi, wlo, nst, nw):
    return eng.tensor_tensor(wlo[:, u % nw, :], stage[:, u % nst, :], whi[:, u % nw, :].bitcast(F32), ALU.subtract)


def w_cols(g, l, k0, col):
    return g.w_in[bass.ds(l, 1), k0 * P:(k0 + 4) * P, col:col + P].rearrange("a (k p) n -> p (a k) n", p=P)


def gate_a_phase(nc, l, g, sem):
    R = Region(nc, "ga", g.free_gate)
    S = lambda n: sem(f"g_{n}")
    NW = NST = KT
    NST = 3
    stage, whi, wlo = R("stage", [P, NST, 512]), R("whi", [P, NW, 512], F32R), R("wlo", [P, NW, 512], F32R)
    th, s2 = R("th", [P, 384]), R("s2", [P, 384])
    NK, NV = 4, 3
    kpg, vpg = R("k", [P, NK, NPG, WA]), R("v", [P, NV, NPG, WA])
    kT = R("kT", [P, 2, PAIRS, PAST])
    prob, probT = R("prob", [64, PAST + 64]), R("probT", [P, 3, 64])
    qbd = R("qbd", [P, PAIRS, DB, 64])
    lp = R("lp", [P, NPG, DB * H])
    later = R("later", [64, PAST])
    newc = R("newc", [H, 64])
    above, ones, nub = R("above", [P, P]), R("ones", [P, P]), R("nub", [64, 64])
    selb, selh, smask = R("selb", [64, DB, 64]), R("selh", [H, 64]), R("smask", [64, DB, 64])
    nmx, sm, rc = R("nmx", [64, 1]), R("sm", [64, 1]), R("rc", [64, 1])
    assert R.at <= g.end, (R.at, g.end)
    zps, kps, qps, pps, vps, dps = g.bank[0:2], g.bank[2:4], g.bank[4], g.bank[5], g.bank[6], g.bank[7]
    blocks = [(j, c) for c in range(len(CHUNKS)) for j in range(PAIRS)]
    plan = [("G",) + blocks[0], ("E",) + blocks[0]]
    for slot in range(DB + 3):
        if slot < DB:
            plan += [("K", slot)]
        if slot + 1 < 10:
            plan += [("G",) + blocks[slot + 1]]
            if slot + 1 < 8:
                plan += [("E",) + blocks[slot + 1]]
        if slot == 0:
            plan += [("D",)]
        if 0 <= slot - 1 < DB:
            plan += [("Q", slot - 1)]
        if 0 <= slot - 3 < DB:
            plan += [("V", slot - 3)]
        if 0 <= slot - 2 < DB:
            plan += [("R", slot - 2)]
    plan += [("E",) + b for b in blocks[8:10]]
    for b in blocks[10:]:
        plan += [("G",) + b, ("E",) + b]
    order, count = {}, {}
    for s in plan:
        order[s] = count.get(s[0], 0)
        count[s[0]] = order[s] + 1

    w_in = [S(f"w{i}") for i in range(NST)]
    w_hi, w_lo = S("whi"), S("wlo")
    pt_in, l_in, k_in, v_in = S("pt"), S("lp"), [S(f"k{i}") for i in range(NK)], [S(f"v{i}") for i in range(NV)]
    cst, zq, qbd_r, d_ps, d_done = S("cst"), S("zq"), S("qbd"), S("dps"), S("dd")
    z_ready, th_r, z_free, a_r, a_hi, a_lo = S("z"), S("th"), S("zf"), S("a"), S("ahi"), S("alo")
    k_ps, kT_r, q_ps, b_r, e_r, p_r, r_ps, pT_r, v_ps, o_r = (S(x) for x in (
        "kps", "kT", "qps", "b", "e", "p", "rps", "pT", "vps", "o"))
    own_v, fills = S("own"), S("fills")

    with nc.Block() as block:
        @block.sync
        def _(sp):
            sp.dma_start(g.pages[:, :], g.page_table[:, :]).then_inc(pt_in, 16)
            sp.wait_ge(pt_in, 16)

            def page(b, i):
                return sp.value_load(g.pages[0:1, NPG * b + i:NPG * b + i + 1], min_val=0, max_val=N_POOL - 1)

            def load_w(u):
                if u >= NST:
                    sp.wait_ge(w_lo, u - NST + 1)
                j, half = divmod(u, 2)
                sp.dma_start(stage[:, u % NST, :].rearrange("p (k n) -> p k n", k=4),
                             w_cols(g, l, 4 * half, C_GA + j * P)).then_inc(w_in[u % NST], 16)

            def load_k(b):
                if b >= NK:
                    sp.wait_ge(k_ps, b - NK + 1)
                for i in range(NPG):
                    sp.dma_start(kpg[:, b % NK, i, :],
                                 g.cache_k[bass.ds(l, 1), bass.ds(page(b, i), 1), :, :]
                                 .rearrange("a c p n -> (a c p) n")).then_inc(k_in[b % NK], 16)

            def load_v(b):
                if b >= NV:
                    sp.wait_ge(v_ps, b - NV + 1)
                for i in range(NPG):
                    sp.dma_start(vpg[:, b % NV, i, :],
                                 g.cache_v[bass.ds(l, 1), bass.ds(page(b, i), 1), :, :]
                                 .rearrange("a c p n -> (a c p) n")).then_inc(v_in[b % NV], 16)

            load_w(0)
            load_w(1)
            load_w(2)
            load_k(0)
            load_w(3)
            for b in range(DB):
                for i in range(NPG):
                    v = page(b, i)
                    sp.dma_start(lp[:, i, b * H:(b + 1) * H],
                                 g.cache_logf[bass.ds(l, 1), bass.ds(v, 1), :, :]
                                 .rearrange("a c p n -> (a c p) n")).then_inc(l_in, 16)
            load_w(4)
            load_k(1)
            load_v(0)
            load_w(5)
            load_k(2)
            load_w(6)
            load_v(1)
            load_w(7)
            load_k(3)
            load_v(2)
            for b in range(NV, DB):
                if b + 1 < DB:
                    load_k(b + 1)
                load_v(b)

        @block.gpsimd
        def _(pool):
            n = [0]

            def link(ins):
                n[0] += 1
                ins.then_inc(cst, 1)
                pool.wait_ge(cst, n[0])

            link(nc.gpsimd.memset(ones[:, :], 1.0))
            link(nc.gpsimd.affine_select(out=above[:, :], in_=ones[:, :], compare_op=ALU.is_gt, fill=0.0, base=0,
                                         pattern=[[-1, P]], channel_multiplier=1))
            link(nc.gpsimd.memset(nub[:, :], -1.0))
            link(nc.gpsimd.affine_select(out=nub[:, :], in_=nub[:, :], compare_op=ALU.is_ge, fill=0.0, base=0,
                                         pattern=[[1, 64]], channel_multiplier=-1))
            link(nc.gpsimd.affine_select(out=nub[:, :].rearrange("p (b t) -> p b t", t=DT),
                                         in_=nub[:, :].rearrange("p (b t) -> p b t", t=DT),
                                         compare_op=ALU.is_ge, fill=0.0, base=0,
                                         pattern=[[-DT, DB], [0, DT]], channel_multiplier=1))
            link(nc.gpsimd.affine_select(out=selh[:, :].rearrange("p (q h) -> p q h", h=H),
                                         in_=ones[0:H, 0:64].rearrange("p (q h) -> p q h", h=H),
                                         compare_op=ALU.is_equal, fill=0.0, base=0,
                                         pattern=[[0, DT], [-1, H]], channel_multiplier=1))
            pool.wait_ge(fills, 2)
            link(nc.gpsimd.affine_select(out=selb[:, :, :].rearrange("p b (q h) -> p b q h", h=H),
                                         in_=selb[:, :, :].rearrange("p b (q h) -> p b q h", h=H),
                                         compare_op=ALU.is_equal, fill=0.0, base=0,
                                         pattern=[[-H, DB], [0, DT], [-1, H]], channel_multiplier=1))
            sm4 = smask[:, :, :].rearrange("p b (c t) -> p b c t", t=DT)
            link(nc.gpsimd.affine_select(out=sm4, in_=sm4, compare_op=ALU.is_equal, fill=NEG, base=0,
                                         pattern=[[-1, DB], [1, DB], [0, DT]], channel_multiplier=0))
            link(nc.gpsimd.affine_select(out=sm4, in_=sm4, compare_op=ALU.is_ge, fill=NEG, base=0,
                                         pattern=[[0, DB], [0, DB], [-H, DT]], channel_multiplier=1))
            pool.sem_inc(zq, 1)
            for bi, (j, c) in enumerate(blocks):
                at, n_ = CHUNKS[c]
                pool.wait_ge(a_hi, bi + 1)
                nc.gpsimd.tensor_tensor(g.a_lo[:, j, at:at + n_], g.a[:, j, at:at + n_],
                                        g.a_hi[:, j, at:at + n_].bitcast(F32), ALU.subtract).then_inc(a_lo, 1)
            pool.wait_ge(a_lo, len(blocks))

        @block.scalar
        def _(act):
            def split(u):
                act.wait_ge(w_in[u % NST], 16 * (u // NST + 1))
                nc.scalar.activation(whi[:, u, :], stage[:, u % NST, :], ACT.Copy).then_inc(w_hi, 1)

            split(0)
            split(1)
            nu = 2
            for s in plan:
                if s[0] == "G":
                    if nu < NW:
                        split(nu)
                        split(nu + 1)
                        nu += 2
                elif s[0] == "D":
                    act.wait_ge(fills, 3)
                    for p in range(PAIRS):
                        for hh in range(2):
                            r = slice(HD * hh, HD * hh + HD)
                            dst = qbd[r, p, :, :].rearrange("p b (q h) -> p b q h", h=H)[:, :, :, 2 * p + hh]
                            src = g.qk_s[r, 0, p, :].rearrange("p (b q) -> p b q", q=DT)
                            nc.scalar.activation(dst, src, ACT.Copy).then_inc(qbd_r, 1)
                elif s[0] == "E":
                    j, c = s[1:]
                    gi = order[s]
                    at, n_ = CHUNKS[c]
                    act.wait_ge(z_ready, gi + 1)
                    if gi:
                        act.wait_ge(z_free, gi)
                    nc.scalar.activation(th[:, 0:n_], zps[gi % 2][:, 0:n_], ACT.Tanh, scale=0.5).then_inc(th_r, 1)
                    act.wait_ge(a_r, gi + 1)
                    nc.scalar.activation(g.a_hi[:, j, at:at + n_], g.a[:, j, at:at + n_], ACT.Copy).then_inc(a_hi, 1)
                elif s[0] == "K":
                    b = s[1]
                    act.wait_ge(k_ps, b + 1)
                    if b >= 2:
                        act.wait_ge(q_ps, b - 1)
                    nc.scalar.activation(kT[:, b % 2, :, 0:P], kps[0][:, :].rearrange("p (c r) -> p c r", c=4), ACT.Copy)
                    nc.scalar.activation(kT[:, b % 2, :, P:2 * P], kps[1][:, :].rearrange("p (c r) -> p c r", c=4),
                                         ACT.Copy).then_inc(kT_r, 1)
                elif s[0] == "Q":
                    b = s[1]
                    act.wait_ge(b_r, b + 1)
                    if b:
                        act.wait_ge(r_ps, b)
                        act.wait_ge(p_r, b)
                    nc.scalar.activation(prob[:, :], qps[0:64, 0:PAST + 64], ACT.Exp, bias=nmx[:, 0:1],
                                         accum_out=sm[:, 0:1]).then_inc(e_r, 1)

        @block.vector
        def _(dve):
            n = [0]

            def link(ins):
                n[0] += 1
                ins.then_inc(own_v, 1)
                dve.wait_ge(own_v, n[0])

            def split_lo(u):
                dve.wait_ge(w_hi, u + 1)
                split_units(nc, nc.vector, u, stage, whi, wlo, NST, NW).then_inc(w_lo, 1)

            split_lo(0)
            split_lo(1)
            nc.vector.memset(selb[:, :, :], 1.0).then_inc(fills, 1)
            nc.vector.memset(smask[:, :, :], 0.0).then_inc(fills, 1)
            nc.vector.memset(qbd[:, :, :, :], 0.0).then_inc(fills, 1)
            nu = 2
            for s in plan:
                if s[0] == "G":
                    if nu < NW:
                        split_lo(nu)
                        split_lo(nu + 1)
                        nu += 2
                elif s[0] == "D":
                    dve.wait_ge(d_ps, 1)
                    nc.vector.tensor_copy(later[:, :], dps[0:64, 0:PAST])
                    nc.vector.tensor_copy(newc[:, :], dps[0:H, PAST:PAST + 64]).then_inc(d_done, 1)
                elif s[0] == "E":
                    j, c = s[1:]
                    gi = order[s]
                    at, n_ = CHUNKS[c]
                    dve.wait_ge(th_r, gi + 1)
                    if c == 2:
                        dve.wait_ge(o_r, DB)
                    nc.vector.scalar_tensor_tensor(s2[:, 0:n_], th[:, 0:n_], 1.0, zps[gi % 2][:, 0:n_],
                                                   ALU.add, ALU.mult).then_inc(z_free, 1)
                    dve.wait_ge(z_free, gi + 1)
                    nc.vector.scalar_tensor_tensor(g.a[:, j, at:at + n_], g.a[:, j, at:at + n_], 0.5, s2[:, 0:n_],
                                                   ALU.mult, ALU.mult).then_inc(a_r, 1)
                    dve.wait_ge(a_r, gi + 1)
                elif s[0] == "Q":
                    b = s[1]
                    dve.wait_ge(q_ps, b + 1)
                    if b:
                        dve.wait_ge(e_r, b)
                    nc.vector.tensor_reduce(nmx[:, :], qps[0:64, 0:PAST + 64], axis=AX.X, op=ALU.max,
                                            negate=True).then_inc(b_r, 1)
                    dve.wait_ge(e_r, b + 1)
                    link(nc.vector.reciprocal(rc[:, :], sm[:, :]))
                    nc.vector.tensor_scalar(prob[:, :], prob[:, :], rc[:, 0:1], None, ALU.mult).then_inc(p_r, 1)
                elif s[0] == "R":
                    b = s[1]
                    dve.wait_ge(r_ps, b + 1)
                    if b:
                        dve.wait_ge(v_ps, b)
                    nc.vector.tensor_copy(probT[:, 0:2, :], pps[:, 0:2 * 64].rearrange("p (g r) -> p g r", g=2))
                    nc.vector.tensor_copy(probT[0:64, 2, :], pps[0:64, 2 * 64:3 * 64]).then_inc(pT_r, 1)
                elif s[0] == "V":
                    b = s[1]
                    dve.wait_ge(v_ps, b + 1)
                    for hh in range(2):
                        r = slice(HD * hh, HD * hh + HD)
                        last = nc.vector.tensor_copy(
                            g.a[r, :, SEQ + DT * b:SEQ + DT * b + DT],
                            vps[r, 0:PAIRS * 16].rearrange("p (c q h) -> p c q h", c=PAIRS, h=2)[:, :, :, hh])
                    last.then_inc(o_r, 1)

        @block.tensor
        def _(pe):
            for s in plan:
                if s[0] == "D":
                    pe.wait_ge(zq, 1)
                    pe.wait_ge(l_in, 16 * DB * NPG)
                    nc.tensor.matmul(dps[0:64, 0:P], lp[:, 0, :], above[:, :], start=True, stop=False)
                    nc.tensor.matmul(dps[0:64, 0:P], lp[:, 1, :], ones[:, :], start=False, stop=True)
                    nc.tensor.matmul(dps[0:64, P:2 * P], lp[:, 1, :], above[:, :], start=True, stop=True)
                    nc.tensor.matmul(dps[0:H, PAST:PAST + 64], g.logf[0:NS_TOK, PT_, :], nub[:, :],
                                     start=True, stop=True).then_inc(d_ps, 1)
                if s[0] == "G":
                    j, c = s[1:]
                    gi = order[s]
                    at, n_ = CHUNKS[c]
                    if gi >= 2:
                        pe.wait_ge(z_free, gi - 1)
                    for k in range(KT):
                        u = 2 * j + k // 4
                        kk = slice((k % 4) * P, (k % 4 + 1) * P)
                        if c == 0:
                            pe.wait_ge(w_lo, u + 1)
                        last = three(nc, zps[gi % 2][:, 0:n_],
                                     [(whi[:, u, kk], wlo[:, u, kk], g.h_hi[:, k, at:at + n_], g.h_lo[:, k, at:at + n_])],
                                     k == 0, k == KT - 1)
                    last.then_inc(z_ready, 1)
                elif s[0] == "K":
                    b = s[1]
                    pe.wait_ge(k_in[b % NK], 16 * NPG * (b // NK + 1))
                    if b:
                        pe.wait_ge(kT_r, b)
                    for i in range(NPG):
                        for p in range(PAIRS):
                            last = nc.tensor.transpose(kps[i][:, p * P:(p + 1) * P],
                                                       kpg[:, b % NK, i, p * P:(p + 1) * P], g.ident[:, :])
                    last.then_inc(k_ps, 1)
                elif s[0] == "Q":
                    b = s[1]
                    pe.wait_ge(kT_r, b + 1)
                    if b == 0:
                        pe.wait_ge(qbd_r, 2 * PAIRS)
                        pe.wait_ge(d_done, 1)
                    else:
                        pe.wait_ge(e_r, b)
                    for p in range(PAIRS):
                        nc.tensor.matmul(qps[0:64, 0:PAST], qbd[:, p, b, :], kT[:, b % 2, p, :], start=p == 0, stop=False)
                    nc.tensor.matmul(qps[0:64, 0:PAST], selb[:, b, :], later[:, :], start=False, stop=True)
                    for p in range(PAIRS):
                        nc.tensor.matmul(qps[0:64, PAST:PAST + 64], qbd[:, p, b, :], g.qk_s[:, 1, p, :],
                                         start=p == 0, stop=False)
                    nc.tensor.matmul(qps[0:64, PAST:PAST + 64], selh[:, :], newc[:, :], start=False, stop=False)
                    nc.tensor.matmul(qps[0:64, PAST:PAST + 64], g.ident[0:64, 0:64], smask[:, b, :],
                                     start=False, stop=True).then_inc(q_ps, 1)
                elif s[0] == "R":
                    b = s[1]
                    pe.wait_ge(p_r, b + 1)
                    if b:
                        pe.wait_ge(pT_r, b)
                    for i in range(NPG):
                        nc.tensor.transpose(pps[:, i * 64:(i + 1) * 64], prob[:, i * P:(i + 1) * P], g.ident[0:64, 0:64])
                    nc.tensor.transpose(pps[0:64, 2 * 64:3 * 64], prob[:, PAST:PAST + 64],
                                        g.ident[0:64, 0:64]).then_inc(r_ps, 1)
                elif s[0] == "V":
                    b = s[1]
                    pe.wait_ge(v_in[b % NV], 16 * NPG * (b // NV + 1))
                    pe.wait_ge(pT_r, b + 1)
                    if b:
                        pe.wait_ge(o_r, b)
                    for p in range(PAIRS):
                        out = vps[:, p * 16:(p + 1) * 16]
                        rhs = lambda rows, i: probT[rows, i, :].rearrange("p (q h) -> p q h", h=H)[:, :, 2 * p:2 * p + 2]
                        for i in range(NPG):
                            nc.tensor.matmul(out, vpg[:, b % NV, i, p * P:(p + 1) * P], rhs(slice(0, P), i),
                                             start=i == 0, stop=False)
                        last = nc.tensor.matmul(out, g.v_s[:, p * P:(p + 1) * P], rhs(slice(0, 64), 2),
                                                start=False, stop=True)
                    last.then_inc(v_ps, 1)


def sgu_phase(nc, l, g, sem):
    R = Region(nc, "sg", g.free_sgu)
    S = lambda n: sem(f"s_{n}")
    NW, NST = KT, 2
    stage, whi, wlo = R("stage", [P, NST, 512]), R("whi", [P, NW, 512], F32R), R("wlo", [P, NW, 512], F32R)
    sT = R("sT", [P, PAIRS, NTOK])
    after = R.at
    fb = R("fb", [P, 2, 384])
    assert R.at <= g.b_at, (R.at, g.b_at)
    Q = Region(nc, "sv", g.b_at)
    b_end = g.b_at + 2 * PAIRS * NTOK * 4
    vh, vl = Q("vh", [P, 2, WA], F32R), Q("vl", [P, 2, WA], F32R)
    ws = Q("ws", [P, H, P])
    w_hi_s, w_lo_s = Q("wshi", [P, H, P], F32R), Q("wslo", [P, H, P], F32R)
    assert Q.at <= b_end, (Q.at, b_end)
    Q2 = Region(nc, "sx", R.at)
    g2, gvb = Q2("g2", [P, WA]), Q2("gvb", [P, WA])
    assert Q2.at <= g.b_at, (Q2.at, g.b_at)
    Q3 = Region(nc, "sy", b_end)
    sqv, thv = Q3("sqv", [P, WA]), Q3("thv", [P, WA])
    vs = Q3("vs", [64, WA])
    bs = Q3("bs", [P, PAIRS, P])
    wb, wbT = Q3("wb", [64, H, 64]), Q3("wbT", [64, H, 64])
    sqc, thc = sqv, thv
    ss, ms, rs, ex = (Q3(x, [P, 1]) for x in ("ss", "ms", "rs", "ex"))
    assert Q3.at <= g.end, (Q3.at, g.end)
    zps, wps, gps = g.bank[0:2], g.bank[2:4], g.bank[4:8]

    u_cols = [("vb", k) for k in range(KT)] + [(C_U + j * P, hf) for j in range(PAIRS) for hf in range(2)] \
        + [(C_GB + j * P, hf) for j in range(PAIRS) for hf in range(2)]
    NU = len(u_cols)
    steps = [("U", j, c) for j in range(PAIRS) for c in range(3)] + [("B", j, c) for j in range(PAIRS) for c in range(3)]

    w_in = [S(f"w{i}") for i in range(NST)]
    w_hi, w_lo, w_lo_v, w_used = S("whi"), S("wlo"), S("wlov"), S("wused")
    cst, cst2, ws_in, wb_z, ws_m, ws_ps, ws_hi, ws_lo, wb_ps, wb_r = (S(x) for x in (
        "cst", "cst2", "ws", "wbz", "wsm", "wsps", "wshi", "wslo", "wbps", "wbr"))
    z_ready, sq_r, w3_r, th_r, g2_r, ss_r, ms_r, rs_r, vb_r, vh_r, vl_r, g_ps, g_r, vb_out = (S(x) for x in (
        "z", "sq", "w3", "th", "g2", "ss", "ms", "rs", "vb", "vh", "vl", "gps", "gr", "vbo"))
    u_z, u_sq, u_w3, u_th, u_g2, u_s, b_r, b_hi, b_lo = (S(x) for x in (
        "uz", "usq", "uw3", "uth", "ug2", "us", "b", "bhi", "blo"))

    def wait_split(eng, u):
        v = min(u + 1, KT) // 2
        if u < KT and u % 2:
            eng.wait_ge(w_lo_v, v)
        else:
            eng.wait_ge(w_lo, u + 1 - v)

    with nc.Block() as block:
        @block.sync
        def _(sp):
            def load_w(u):
                if u >= NST:
                    wait_split(sp, u - NST)
                col, hf = u_cols[u]
                if col == "vb":
                    sp.dma_start(stage[:, u % NST, :],
                                 g.w_in[bass.ds(l, 1), hf * P:(hf + 1) * P, C_VB:C_VB + WA]
                                 .rearrange("a p n -> (a p) n")).then_inc(w_in[u % NST], 16)
                else:
                    sp.dma_start(stage[:, u % NST, :].rearrange("p (k n) -> p k n", k=4),
                                 w_cols(g, l, 4 * hf, col)).then_inc(w_in[u % NST], 16)

            load_w(0)
            load_w(1)
            for u in range(2, KT):
                load_w(u)
            sp.dma_start(ws[:, :, :], g.w_s[bass.ds(l, 1), :, :, :].rearrange("a g t s -> t (a g) s")).then_inc(ws_in, 16)
            sp.dma_start(gvb[:, :], g.v_norm_g[bass.ds(l, 1), :].to_broadcast([P, WA])).then_inc(cst, 16)
            for p in range(PAIRS):
                for hh in range(2):
                    sp.dma_start(bs[HD * hh:HD * hh + HD, p, :],
                                 g.b_s[bass.ds(l, 1), 2 * p + hh, :].to_broadcast([HD, P])).then_inc(cst, 16)
            sp.wait_ge(wb_z, 1)
            for b in range(DB):
                sp.dma_start(wb[DT * b:DT * b + DT, :, DT * b:DT * b + DT],
                             g.w_s[bass.ds(l, 1), :, 0:DT, 0:DT].rearrange("a g t s -> t (a g) s")).then_inc(cst2, 16)
            for u in range(KT, NU):
                if u == KT + NST:
                    sp.wait_ge(vb_r, NT)
                    sp.dma_start(g.nsv[bass.ds(l, 1), :, :].rearrange("a p n -> (a p) n"), vs[:, :]).then_inc(vb_out, 16)
                load_w(u)
            sp.wait_ge(vb_out, 16)

        @block.scalar
        def _(act):
            def split(u):
                act.wait_ge(w_in[u % NST], 16 * (u // NST + 1))
                v = u - NW
                if 0 <= v < KT - 1:
                    act.wait_ge(w_used, v + 1)
                elif v == KT - 1:
                    act.wait_ge(z_ready, NT)
                elif v >= KT:
                    blk, half = divmod(v - KT, 2)
                    if half == 0:
                        act.wait_ge(w_used, KT + blk)
                    else:
                        act.wait_ge(u_z, 3 * (blk + 1))
                nc.scalar.activation(whi[:, u % NW, :], stage[:, u % NST, :], ACT.Copy).then_inc(w_hi, 1)

            for u in range(KT):
                split(u)
            act.wait_ge(cst, 144)
            nc.scalar.activation(gvb[:, :], gvb[:, :], ACT.Copy, scale=0.5).then_inc(ws_m, 1)
            for t in range(NT):
                n = ROWS[t]
                if t == 1:
                    for i in range(2):
                        act.wait_ge(ws_ps, i + 1)
                        nc.scalar.activation(w_hi_s[:, 4 * i:4 * i + 4, :],
                                             wps[i][:, :].rearrange("p (g t) -> p g t", g=4), ACT.Copy).then_inc(ws_hi, 1)
                    act.wait_ge(wb_ps, 1)
                    nc.scalar.activation(wbT[:, :, :], gps[0][0:64, :].rearrange("p (g t) -> p g t", g=H),
                                         ACT.Copy).then_inc(wb_r, 1)
                z = zps[t % 2][0:n, :]
                act.wait_ge(z_ready, t + 1)
                if t:
                    act.wait_ge(w3_r, t)
                    act.wait_ge(g2_r, t)
                    act.wait_ge(ss_r, t)
                nc.scalar.activation(sqv[0:n, :], z, ACT.Square).then_inc(sq_r, 1)
                act.wait_ge(w3_r, t + 1)
                nc.scalar.activation(thv[0:n, :], sqv[0:n, :], ACT.Tanh, scale=GC * GS).then_inc(th_r, 1)
                act.wait_ge(g2_r, t + 1)
                act.wait_ge(th_r, t + 1)
                if t:
                    act.wait_ge(ms_r, t)
                nc.scalar.activation(thv[0:n, :], g2[0:n, :], ACT.Square, scale=0.5, accum_out=ss[0:n, :]).then_inc(ss_r, 1)
                if t < PT_:
                    act.wait_ge(vb_r, t + 1)
                    if t >= 2:
                        act.wait_ge(g_ps, t - 1)
                    nc.scalar.activation(vh[:, t % 2, :], g2[:, :], ACT.Copy).then_inc(vh_r, 1)
            for i, (kind, j, c) in enumerate(steps):
                at, n = CHUNKS[c]
                z = zps[i % 2][:, 0:n]
                if c == 0 and kind == "U" and j == 0:
                    for u in range(KT, KT + 4):
                        split(u)
                if c == 1:
                    for u in ((KT + 2 * (i // 3) + 4), (KT + 2 * (i // 3) + 5)):
                        if u < NU:
                            split(u)
                act.wait_ge(u_z, i + 1)
                if kind == "U":
                    if i:
                        act.wait_ge(u_w3, i)
                        act.wait_ge(u_th, i)
                    else:
                        act.wait_ge(g2_r, NT)
                        act.wait_ge(ss_r, NT)
                    nc.scalar.activation(sqc[:, 0:n], z, ACT.Square).then_inc(u_sq, 1)
                    act.wait_ge(u_w3, i + 1)
                    if i:
                        act.wait_ge(u_s, i)
                    nc.scalar.activation(thc[:, 0:n], sqc[:, 0:n], ACT.Tanh, scale=GC * GS).then_inc(u_th, 1)
                else:
                    bi = i - len(steps) // 2
                    if bi:
                        act.wait_ge(b_r, bi)
                    else:
                        act.wait_ge(u_s, len(steps) // 2)
                    nc.scalar.activation(thc[:, 0:n], z, ACT.Tanh, scale=0.5).then_inc(u_th, 1)
                    act.wait_ge(b_r, bi + 1)
                    nc.scalar.activation(g.b_hi[:, j, at:at + n], fb[:, bi % 2, 0:n], ACT.Copy).then_inc(b_hi, 1)

        @block.gpsimd
        def _(pool):
            n_ = [0]
            own = S("pown")

            def link(ins):
                n_[0] += 1
                ins.then_inc(own, 1)
                pool.wait_ge(own, n_[0])

            nc.gpsimd.memset(wb[:, :, :], 0.0).then_inc(wb_z, 1)
            link(nc.gpsimd.memset(ex[:, :], -0.5))
            for u in range(0, KT, 2):
                pool.wait_ge(w_hi, u + 1)
                split_units(nc, nc.gpsimd, u, stage, whi, wlo, NST, NW).then_inc(w_lo, 1)
            pool.wait_ge(ws_in, 16)
            link(nc.gpsimd.affine_select(out=ws[:, :, :], in_=ws[:, :, :], compare_op=ALU.is_ge, fill=0.0, base=0,
                                         pattern=[[0, H], [-1, P]], channel_multiplier=1))
            pool.wait_ge(cst2, 16 * DB)
            link(nc.gpsimd.affine_select(out=wb[:, :, :], in_=wb[:, :, :], compare_op=ALU.is_ge, fill=0.0, base=0,
                                         pattern=[[0, H], [-1, 64]], channel_multiplier=1))
            pool.sem_inc(ws_m, 1)
            for t in range(NT):
                pool.wait_ge(ms_r, t + 1)
                if t:
                    pool.wait_ge(vb_r, t)
                nc.gpsimd.tensor_tensor(rs[0:ROWS[t], :], ms[0:ROWS[t], :], ex[0:ROWS[t], :], ALU.pow).then_inc(rs_r, 1)
            for u in range(KT, KT + 4):
                pool.wait_ge(w_hi, u + 1)
                split_units(nc, nc.gpsimd, u, stage, whi, wlo, NST, NW).then_inc(w_lo, 1)
            for i, (kind, j, c) in enumerate(steps):
                at, n = CHUNKS[c]
                if c == 1:
                    for u in ((KT + 2 * (i // 3) + 4), (KT + 2 * (i // 3) + 5)):
                        if u < NU:
                            pool.wait_ge(w_hi, u + 1)
                            split_units(nc, nc.gpsimd, u, stage, whi, wlo, NST, NW).then_inc(w_lo, 1)
                if kind == "B":
                    bi = i - len(steps) // 2
                    pool.wait_ge(b_hi, bi + 1)
                    nc.gpsimd.tensor_tensor(g.b_lo[:, j, at:at + n], fb[:, bi % 2, 0:n],
                                            g.b_hi[:, j, at:at + n].bitcast(F32), ALU.subtract).then_inc(b_lo, 1)
            pool.wait_ge(b_lo, len(steps) // 2)

        @block.vector
        def _(dve):
            def split_lo(u):
                dve.wait_ge(w_hi, u + 1)
                split_units(nc, nc.vector, u, stage, whi, wlo, NST, NW).then_inc(w_lo_v, 1)

            def gating(t):
                dve.wait_ge(g_ps, t + 1)
                if t < PT_:
                    for p in range(PAIRS):
                        for hh in range(2):
                            r = slice(HD * hh, HD * hh + HD)
                            at = 256 * (p % 2) + P * hh
                            last = nc.vector.tensor_tensor(sT[r, p, t * P:(t + 1) * P],
                                                           gps[2 * (t % 2) + p // 2][r, at:at + P], bs[r, p, :], ALU.add)
                else:
                    for p in range(PAIRS):
                        for hh in range(2):
                            r = slice(HD * hh, HD * hh + HD)
                            last = nc.vector.tensor_tensor(
                                sT[r, p, SEQ:NTOK].rearrange("p (b t) -> p b t", t=DT),
                                gps[2 * (t % 2)][r, P * p + 64 * hh:P * p + 64 * hh + 64].rearrange("p (b t) -> p b t", t=DT),
                                bs[r, p, 0:DT].unsqueeze(1).to_broadcast([HD, DB, DT]), ALU.add)
                last.then_inc(g_r, 1)

            for u in range(1, KT, 2):
                split_lo(u)
            dve.wait_ge(ws_m, 2)
            for t in range(NT):
                n = ROWS[t]
                if t == 1:
                    for i in range(2):
                        dve.wait_ge(ws_hi, i + 1)
                        nc.vector.tensor_tensor(w_lo_s[:, 4 * i:4 * i + 4, :], wps[i][:, :].rearrange("p (g t) -> p g t", g=4),
                                                w_hi_s[:, 4 * i:4 * i + 4, :].bitcast(F32), ALU.subtract).then_inc(ws_lo, 1)
                z = zps[t % 2][0:n, :]
                dve.wait_ge(sq_r, t + 1)
                nc.vector.scalar_tensor_tensor(sqv[0:n, :], sqv[0:n, :], 1.0 / GC, z, ALU.add, ALU.mult).then_inc(w3_r, 1)
                dve.wait_ge(th_r, t + 1)
                if t:
                    dve.wait_ge(vl_r, min(t, PT_))
                nc.vector.scalar_tensor_tensor(g2[0:n, :], thv[0:n, :], 1.0, z, ALU.add, ALU.mult).then_inc(g2_r, 1)
                if t:
                    gating(t - 1)
                dve.wait_ge(ss_r, t + 1)
                nc.vector.tensor_scalar(ms[0:n, :], ss[0:n, :], 1.0 / WA, EPS, ALU.mult, ALU.add).then_inc(ms_r, 1)
                dve.wait_ge(rs_r, t + 1)
                nc.vector.scalar_tensor_tensor(g2[0:n, :] if t < PT_ else vs[:, :], g2[0:n, :], rs[0:n, 0:1],
                                               gvb[0:n, :], ALU.mult, ALU.mult).then_inc(vb_r, 1)
                if t < PT_:
                    dve.wait_ge(vh_r, t + 1)
                    nc.vector.tensor_tensor(vl[:, t % 2, :], g2[:, :], vh[:, t % 2, :].bitcast(F32),
                                            ALU.subtract).then_inc(vl_r, 1)
            gating(NT - 1)
            dve.wait_ge(g_r, NT)
            for i, (kind, j, c) in enumerate(steps):
                at, n = CHUNKS[c]
                z = zps[i % 2][:, 0:n]
                s = sT[:, j, at:at + n]
                if kind == "U":
                    dve.wait_ge(u_sq, i + 1)
                    nc.vector.scalar_tensor_tensor(sqc[:, 0:n], sqc[:, 0:n], 1.0 / GC, z, ALU.add, ALU.mult).then_inc(u_w3, 1)
                dve.wait_ge(u_th, i + 1)
                bi = i - len(steps) // 2
                nc.vector.scalar_tensor_tensor(thc[:, 0:n], thc[:, 0:n], 1.0, z, ALU.add, ALU.mult).then_inc(u_g2, 1)
                dve.wait_ge(u_g2, i + 1)
                if kind == "U":
                    nc.vector.scalar_tensor_tensor(s, thc[:, 0:n], 0.25, s, ALU.mult, ALU.mult).then_inc(u_s, 1)
                else:
                    dve.wait_ge(u_s, len(steps) // 2)
                    if bi >= 2:
                        dve.wait_ge(b_lo, bi - 1)
                    nc.vector.tensor_tensor(fb[:, bi % 2, 0:n], thc[:, 0:n], s, ALU.mult).then_inc(b_r, 1)
                dve.wait_ge(b_r if kind == "B" else u_s, bi + 1 if kind == "B" else i + 1)

        @block.tensor
        def _(pe):
            def spatial_weights():
                pe.wait_ge(ws_m, 2)
                for i in range(2):
                    for k in range(4):
                        last = nc.tensor.transpose(wps[i][:, k * P:(k + 1) * P], ws[:, 4 * i + k, :], g.ident[:, :])
                    last.then_inc(ws_ps, 1)
                for k in range(H):
                    last = nc.tensor.transpose(gps[0][0:64, 64 * k:64 * k + 64], wb[:, k, :], g.ident[0:64, 0:64])
                last.then_inc(wb_ps, 1)

            def gating(t):
                if t >= 2:
                    pe.wait_ge(g_r, t - 1)
                if t < PT_:
                    pe.wait_ge(vl_r, t + 1)
                    if t == 0:
                        pe.wait_ge(ws_lo, 2)
                        pe.wait_ge(wb_r, 1)
                    for p in range(PAIRS):
                        cols = slice(p * P, (p + 1) * P)
                        last = three(nc, gps[2 * (t % 2) + p // 2][:, 256 * (p % 2):256 * (p % 2) + 256],
                                     [(vh[:, t % 2, cols], vl[:, t % 2, cols],
                                       w_hi_s[:, 2 * p:2 * p + 2, :], w_lo_s[:, 2 * p:2 * p + 2, :])], True, True)
                else:
                    pe.wait_ge(vb_r, NT)
                    for p in range(PAIRS):
                        last = nc.tensor.matmul(gps[2 * (t % 2)][:, P * p:P * p + P], vs[:, p * P:(p + 1) * P],
                                                wbT[:, 2 * p:2 * p + 2, :], start=True, stop=True)
                last.then_inc(g_ps, 1)

            for t in range(NT):
                n = ROWS[t]
                r = slice(t * P, t * P + n)
                if t >= 2:
                    pe.wait_ge(g2_r, t - 1)
                for k in range(KT):
                    if t == 0:
                        wait_split(pe, k)
                    last = three(nc, zps[t % 2][0:n, :],
                                 [(g.h_hi[:, k, r], g.h_lo[:, k, r], whi[:, k, :], wlo[:, k, :])], k == 0, k == KT - 1)
                    if t == NT - 1 and k < KT - 1:
                        last.then_inc(w_used, 1)
                last.then_inc(z_ready, 1)
                if t == 1:
                    spatial_weights()
                elif t:
                    gating(t - 2)
            gating(NT - 2)
            for i, (kind, j, c) in enumerate(steps):
                at, n = CHUNKS[c]
                if i < 2:
                    pe.wait_ge(g2_r, NT)
                else:
                    pe.wait_ge(u_g2, i - 1)
                for k in range(KT):
                    u = KT + 2 * (i // 3) + k // 4
                    kk = slice((k % 4) * P, (k % 4 + 1) * P)
                    if c == 0:
                        wait_split(pe, u)
                    last = three(nc, zps[i % 2][:, 0:n],
                                 [(whi[:, u % NW, kk], wlo[:, u % NW, kk], g.h_hi[:, k, at:at + n], g.h_lo[:, k, at:at + n])],
                                 k == 0, k == KT - 1)
                    if c == 2 and k == 3:
                        last.then_inc(w_used, 1)
                last.then_inc(u_z, 1)
                if i == 0:
                    gating(NT - 1)


def merge_phase(nc, l, g, sem):
    R = Region(nc, "me", g.free_merge)
    S = lambda n: sem(f"m_{n}")
    NW, NST = 6, 3
    stage, whi, wlo = R("stage", [P, NST, 512]), R("whi", [P, NW, 512], F32R), R("wlo", [P, NW, 512], F32R)
    ta, tb = R("ta", [P, 384]), R("tb", [P, 384])
    assert R.at <= g.end, (R.at, g.end)
    PER = 6
    NU = KT * PER
    steps = [(j, c) for j in range(KT) for c in range(3)]
    w_in = [S(f"w{i}") for i in range(NST)]
    w_hi, w_lo_p, w_lo_v, w_used = S("whi"), S("wlop"), S("wlov"), S("wused")
    z_ready, t_r, p_ready, m_a, m_b, m_r = S("z"), S("t"), S("p"), S("ma"), S("mb"), S("mr")

    def lo_count(u):
        v = (u + 1) // 3
        return u + 1 - v, v

    with nc.Block() as block:
        @block.sync
        def _(sp):
            for u in range(NU):
                j, x = divmod(u, PER)
                if u >= NST:
                    a, b = lo_count(u - NST)
                    sp.wait_ge(w_lo_p, a)
                    if b:
                        sp.wait_ge(w_lo_v, b)
                if x < 4:
                    src = w_cols(g, l, 4 * (x % 2), (C_MA if x < 2 else C_MB) + j * P)
                else:
                    w = g.w_pa if x == 4 else g.w_pb
                    src = w[bass.ds(l, 1), :, j * P:(j + 1) * P].rearrange("a (k p) n -> p (a k) n", p=P)
                sp.dma_start(stage[:, u % NST, :].rearrange("p (k n) -> p k n", k=4), src).then_inc(w_in[u % NST], 16)

        def split_after(i):
            j, c = steps[i]
            return range(PER * (j + 1), min(PER * (j + 2), NU)) if c == 2 else range(0)

        @block.scalar
        def _(act):
            def split(u):
                act.wait_ge(w_in[u % NST], 16 * (u // NST + 1))
                if u >= NW:
                    j, x = divmod(u - NW, PER)
                    if x in (0, 2):
                        act.wait_ge(w_used, 2 * j + x // 2 + 1)
                    elif x < 4:
                        act.wait_ge(z_ready, 6 * j + 5 + x // 2)
                    else:
                        act.wait_ge(p_ready, 6 * j + 1 + x)
                nc.scalar.activation(whi[:, u % NW, :], stage[:, u % NST, :], ACT.Copy).then_inc(w_hi, 1)

            for u in range(PER):
                split(u)
            for i, (j, c) in enumerate(steps):
                at, n = CHUNKS[c]
                b = 4 * (i % 2)
                for x, t in ((0, ta), (1, tb)):
                    if c == 2 and x == 0:
                        pass
                    act.wait_ge(z_ready, 2 * i + x + 1)
                    if i:
                        act.wait_ge(m_a if x == 0 else m_b, i)
                    nc.scalar.activation(t[:, 0:n], g.bank[b + x][:, 0:n], ACT.Tanh, scale=0.5).then_inc(t_r, 1)
                for u in split_after(i):
                    split(u)

        @block.gpsimd
        def _(pool):
            def lo(u):
                if u % 3 != 2:
                    pool.wait_ge(w_hi, u + 1)
                    split_units(nc, nc.gpsimd, u, stage, whi, wlo, NST, NW).then_inc(w_lo_p, 1)

            for u in range(PER):
                lo(u)
            for i in range(len(steps)):
                for u in split_after(i):
                    lo(u)

        @block.vector
        def _(dve):
            def lo(u):
                if u % 3 == 2:
                    dve.wait_ge(w_hi, u + 1)
                    split_units(nc, nc.vector, u, stage, whi, wlo, NST, NW).then_inc(w_lo_v, 1)

            for u in range(PER):
                lo(u)
            for i, (j, c) in enumerate(steps):
                at, n = CHUNKS[c]
                b = 4 * (i % 2)
                m = g.m[:, j, at:at + n]
                dve.wait_ge(t_r, 2 * i + 1)
                dve.wait_ge(p_ready, 2 * i + 1)
                nc.vector.scalar_tensor_tensor(m, ta[:, 0:n], 1.0, g.bank[b + 2][:, 0:n], ALU.add, ALU.mult).then_inc(m_a, 1)
                dve.wait_ge(t_r, 2 * i + 2)
                dve.wait_ge(p_ready, 2 * i + 2)
                nc.vector.scalar_tensor_tensor(tb[:, 0:n], tb[:, 0:n], 1.0, g.bank[b + 3][:, 0:n],
                                               ALU.add, ALU.mult).then_inc(m_r, 1)
                dve.wait_ge(m_a, i + 1)
                dve.wait_ge(m_r, i + 1)
                nc.vector.tensor_tensor(m, m, tb[:, 0:n], ALU.add).then_inc(m_b, 1)
                for u in split_after(i):
                    lo(u)
            dve.wait_ge(m_b, len(steps))

        @block.tensor
        def _(pe):
            for i, (j, c) in enumerate(steps):
                at, n = CHUNKS[c]
                b = 4 * (i % 2)
                rows = slice(at, at + n)

                def wait_w(u):
                    if c == 0:
                        x, v = lo_count(u)
                        pe.wait_ge(w_lo_p, x)
                        if v:
                            pe.wait_ge(w_lo_v, v)

                if i >= 2:
                    pe.wait_ge(m_b, i - 1)
                for x in range(2):
                    for k in range(KT):
                        u = PER * j + 2 * x + k // 4
                        kk = slice((k % 4) * P, (k % 4 + 1) * P)
                        if k % 4 == 0:
                            wait_w(u)
                        last = three(nc, g.bank[b + x][:, 0:n],
                                     [(whi[:, u % NW, kk], wlo[:, u % NW, kk], g.h_hi[:, k, rows], g.h_lo[:, k, rows])],
                                     k == 0, k == KT - 1)
                        if c == 2 and k == 3:
                            last.then_inc(w_used, 1)
                    last.then_inc(z_ready, 1)
                for x, (hi, lo) in enumerate(((g.a_hi, g.a_lo), (g.b_hi, g.b_lo))):
                    u = PER * j + 4 + x
                    wait_w(u)
                    for k in range(4):
                        kk = slice(k * P, (k + 1) * P)
                        last = three(nc, g.bank[b + 2 + x][:, 0:n],
                                     [(whi[:, u % NW, kk], wlo[:, u % NW, kk], hi[:, k, rows], lo[:, k, rows])],
                                     k == 0, k == 3)
                    last.then_inc(p_ready, 1)


class State:
    pass


def constants_phase(nc, norm_g, g, sem):
    made, gains_in = sem("made"), sem("gains_in")
    mask = nc.alloc_sbuf_tensor_at("mask", [P, P], F32, offset=g.free)
    with nc.Block() as block:
        @block.sync
        def _(sp):
            sp.dma_start(g.gains[0:DEPTH, :], norm_g[:, :]).then_inc(gains_in, 16)
            sp.dma_start(g.gains[DEPTH:DEPTH + 1, :], norm_g[0:1, :]).then_inc(gains_in, 16)
            sp.wait_ge(gains_in, 32)

        @block.gpsimd
        def _(pool):
            nc.gpsimd.memset(g.ident[:, :], 0.0).then_inc(made, 1)
            nc.gpsimd.memset(mask[:, :], 0.0).then_inc(made, 1)
            pool.wait_ge(made, 2)
            nc.gpsimd.affine_select(out=g.ident[:, :], in_=g.ident[:, :], compare_op=ALU.not_equal, fill=1.0,
                                    base=0, pattern=[[-1, P]], channel_multiplier=1).then_inc(made, 1)
            nc.gpsimd.affine_select(out=mask[:, :], in_=mask[:, :], compare_op=ALU.is_ge, fill=NEG,
                                    base=0, pattern=[[-1, P]], channel_multiplier=1).then_inc(made, 1)

        @block.scalar
        def _(act):
            act.wait_ge(made, 4)
            nc.scalar.activation(g.ident_r[:, :], g.ident[:, :], ACT.Copy)
            nc.scalar.activation(g.mask_r[:, :], mask[:, :], ACT.Copy)


def program(nc, x_prompt, x_sample, cache_k, cache_v, cache_logf, page_table, norm_g, w_in, b_forget, q_norm_g,
            k_norm_g, v_norm_g, w_s, b_s, w_proj_a, w_proj_b, w_out,
            y_prompt, y_sample, nkp, nvp, nlp, nks, nvs, nls, nsv):
    g = State()
    g.xp2 = x_prompt.rearrange("a s d -> (a s) d")
    g.xs2 = x_sample.rearrange("a s d -> (a s) d")
    g.yp2 = y_prompt.rearrange("a s d -> (a s) d")
    g.ys2 = y_sample.rearrange("a s d -> (a s) d")
    g.cache_k = cache_k.rearrange("l n s h d -> l n s (h d)")
    g.cache_v = cache_v.rearrange("l n s h d -> l n s (h d)")
    g.cache_logf = cache_logf
    g.page_table = page_table.rearrange("(a b) n -> a (b n)", a=1)
    g.w_in, g.b_forget, g.q_norm_g, g.k_norm_g, g.v_norm_g = w_in, b_forget, q_norm_g, k_norm_g, v_norm_g
    g.w_s, g.b_s, g.w_pa, g.w_pb, g.w_out = w_s, b_s, w_proj_a, w_proj_b, w_out
    g.nkp = nkp.rearrange("l a s h d -> l (a s) (h d)")
    g.nvp = nvp.rearrange("l a s h d -> l (a s) (h d)")
    g.nlp = nlp.rearrange("l a s h -> l (a s) h")
    g.nks = nks.rearrange("l a s h d -> l (a s) (h d)")
    g.nvs = nvs.rearrange("l a s h d -> l (a s) (h d)")
    g.nls = nls.rearrange("l a s h -> l (a s) h")
    g.nsv = nsv.rearrange("l a s w -> l (a s) w")
    g.gains = nc.dram_tensor("gains", (DEPTH + 1, D), F32, kind="Internal").ap()
    g.ncum_dram = nc.dram_tensor("ncum", (H, SEQ), F32, kind="Internal").ap()

    ctx = ExitStack()
    with ctx:
        def phase(build, *args):
            with ExitStack() as own:
                sems = []

                def sem(name):
                    sems.append(own.enter_context(nc.semaphore(name)))
                    return sems[-1]

                build(*args, sem)
                nums = sorted(s.num for s in sems)
                runs = [n for n in nums if n - 1 not in nums]
                with nc.Block() as block:
                    @block.gpsimd
                    def _(pool):
                        for first in runs:
                            last = first
                            while last + 1 in nums:
                                last += 1
                            pool.sem_clear(range(first, last + 1))

        g.end = nc.sbuf_base + nc.sbuf_bytes_remaining
        g.end -= g.end % 32
        K = Region(nc, "keep", (nc.sbuf_base + 31) // 32 * 32)
        g.h_hi, g.h_lo = K("hhi", [P, KT, NTOK], F32R), K("hlo", [P, KT, NTOK], F32R)
        g.ident, g.ident_r, g.mask_r = K("ident", [P, P]), K("identr", [P, P], F32R), K("maskr", [P, P], F32R)
        g.pages = K("pages", [1, DB * NPG], I32)
        g.free = K.at
        A = Region(nc, "keepa", K.at)
        g.logf = A("logf", [P, NT, H])
        g.qk_s = A("qks", [P, 2, PAIRS, NS_TOK])
        g.v_s = A("vs", [NS_TOK, WA])
        g.a = A("a", [P, PAIRS, NTOK])
        g.free_attention = A.at
        ab = 2 * PAIRS * NTOK * 4
        E = Region(nc, "end", g.end - ab)
        g.a_hi, g.a_lo = E("ahi", [P, PAIRS, NTOK], F32R), E("alo", [P, PAIRS, NTOK], F32R)
        g.full_end = g.end
        g.b_at = g.end - 2 * ab - 13 * 1024
        B = Region(nc, "endb", g.b_at)
        g.b_hi, g.b_lo = B("bhi", [P, PAIRS, NTOK], F32R), B("blo", [P, PAIRS, NTOK], F32R)
        g.m = Region(nc, "m", K.at)("m", [P, KT, NTOK])
        g.free_rows = K.at + KT * NTOK * 4
        g.free_merge = None
        g.bank = [ctx.enter_context(nc.psum_tensor(f"bank{i}", [P, 512], F32)) for i in range(8)]

        phase(constants_phase, nc, norm_g, g)
        phase(rows_phase, nc, None, g, False)
        end = g.end
        with nc.Fori(0, DEPTH) as l:
            phase(attention_phase, nc, l, g)
            g.end = end - ab
            g.free_gate = g.free_attention
            phase(gate_a_phase, nc, l, g)
            g.free_sgu = g.free
            phase(sgu_phase, nc, l, g)
            g.free_merge = g.free_rows
            g.end = g.b_at
            phase(merge_phase, nc, l, g)
            g.end = end
            phase(rows_phase, nc, l, g, True)


_INS = ["x_prompt", "x_sample", "cache_k", "cache_v", "cache_logf", "page_table", "norm_g", "w_in", "b_forget",
        "q_norm_g", "k_norm_g", "v_norm_g", "w_s", "b_s", "w_proj_a", "w_proj_b", "w_out"]
_OUTS = [(1, SEQ, D), (DB, DT, D), (DEPTH, 1, SEQ, H, HD), (DEPTH, 1, SEQ, H, HD), (DEPTH, 1, SEQ, H),
         (DEPTH, DB, DT, H, HD), (DEPTH, DB, DT, H, HD), (DEPTH, DB, DT, H), (DEPTH, DB, DT, WA)]


def kernel(**inputs):
    import numpy as np
    import concourse.bacc as bacc
    from concourse.bass_utils import run_bass_kernel_spmd

    nc = bacc.Bacc("TRN2", target_bir_lowering=False, num_devices=1, dynamic_dma_scratch_size=1024)
    arrays, args = {}, []
    for name in _INS:
        a = np.ascontiguousarray(inputs[name])
        arrays[f"in_{name}"] = a
        args.append(nc.dram_tensor(f"in_{name}", a.shape, mybir.dt.from_np(a.dtype), kind="ExternalInput").ap())
    for i, shape in enumerate(_OUTS):
        args.append(nc.dram_tensor(f"out_{i}", shape, F32, kind="ExternalOutput").ap())
    program(nc, *args)
    r = run_bass_kernel_spmd(nc, [arrays], core_ids=[0])
    return tuple(r.results[0][f"out_{i}"] for i in range(len(_OUTS)))
```
